# Optimizing a Trainium2 kernel written in Bass

```python
import math
import jax, jax.numpy as jnp
from jax import lax
import numpy as np

D_MODEL = 1024
BATCH = 1
SEQ = 256
DEPTH = 2

CHUNK = 64
EPS = 1e-6
N_BRANCHES = 2
D_CONV = D_MODEL
CONV_KERNEL = 31
D_POOL = D_MODEL
POOL_WINDOWS = (2, 4, 8, 16)
N_POOL_GROUPS = len(POOL_WINDOWS)
POOL_GROUP = D_POOL // N_POOL_GROUPS
D_IN = 2 * D_CONV + D_POOL + N_BRANCHES * D_MODEL
N_MOD = 6
PEER_HEADS = 8
PEER_NKEYS = 128
PEER_EXPERTS = PEER_NKEYS * PEER_NKEYS
PEER_DKEY = 256
PEER_DHALF = PEER_DKEY // 2
PEER_TOPK = 16
PEER_BLOCK = 128

kernel_name = "hybrid_gated_conv_pool_peer_encoder"

def _rmsnorm(x, g):
    x32 = x.astype(jnp.float32)
    y = x32 * lax.rsqrt(jnp.mean(x32 * x32, axis=-1, keepdims=True) + EPS)
    return (y * g.astype(jnp.float32)).astype(x.dtype)

def _modulate(h, shift, scale):
    return h * (1 + scale[:, None, :]) + shift[:, None, :]

def _conv_branch(val, gate, conv_w, conv_b, ln_g, ln_b, w_co):
    u = val * jax.nn.sigmoid(gate)
    u = lax.conv_general_dilated(
        u, conv_w[:, None, :], window_strides=(1,),
        padding=[(CONV_KERNEL - 1, 0)],
        dimension_numbers=("NWC", "WIO", "NWC"),
        feature_group_count=D_CONV) + conv_b
    u32 = u.astype(jnp.float32)
    mu = jnp.mean(u32, axis=-1, keepdims=True)
    var = jnp.mean(jnp.square(u32 - mu), axis=-1, keepdims=True)
    u = ((u32 - mu) * lax.rsqrt(var + EPS) * ln_g.astype(jnp.float32)
         + ln_b.astype(jnp.float32)).astype(val.dtype)
    return jax.nn.silu(u) @ w_co

def _causal_pool(p):
    B, S, _ = p.shape
    p32 = p.astype(jnp.float32)
    csp = jnp.concatenate([jnp.zeros((B, 1, D_POOL), jnp.float32), jnp.cumsum(p32, axis=1)], axis=1)
    t = jnp.arange(S)
    outs = []
    for g, w in enumerate(POOL_WINDOWS):
        lo, hi = g * POOL_GROUP, (g + 1) * POOL_GROUP
        sl = csp[..., lo:hi]
        upper = sl[:, 1:]
        lower = jnp.concatenate([jnp.zeros((B, w - 1, POOL_GROUP), jnp.float32), sl[:, :S + 1 - w]], axis=1)
        cnt = jnp.minimum(t + 1, w).astype(jnp.float32)
        outs.append((upper - lower) / cnt[None, :, None] - p32[..., lo:hi])
    return jnp.stack(outs, axis=2).astype(p.dtype)

def _peer(h, wq, keys, u_tab, v_tab):
    B, S, D = h.shape
    tokens = h.reshape(-1, PEER_BLOCK, D)

    def block(ht):
        T = ht.shape[0]
        q = (ht @ wq).reshape(T, PEER_HEADS, 2, PEER_DHALF)
        s = jnp.einsum("thpk,hpnk->thpn", q, keys).astype(jnp.float32)
        sv, si = lax.top_k(s, PEER_TOPK)
        cand = sv[:, :, 0, :, None] + sv[:, :, 1, None, :]
        cv, ci = lax.top_k(cand.reshape(T, PEER_HEADS, PEER_TOPK * PEER_TOPK), PEER_TOPK)
        i1 = jnp.take_along_axis(si[:, :, 0], ci // PEER_TOPK, axis=-1)
        i2 = jnp.take_along_axis(si[:, :, 1], ci % PEER_TOPK, axis=-1)
        expert = i1 * PEER_NKEYS + i2
        gw = jax.nn.softmax(cv, axis=-1).astype(ht.dtype)
        u_sel = u_tab[expert]
        v_sel = v_tab[expert]
        act = jax.nn.gelu(jnp.einsum("thkd,td->thk", u_sel, ht), approximate=False)
        return jnp.einsum("thk,thkd->td", gw * act, v_sel)

    return lax.map(block, tokens).reshape(B, S, D)

def setup_inputs(seed: int = 0) -> dict:
    key = jax.random.key(seed)
    ks = jax.random.split(key, 24)
    f32 = jnp.float32
    L, D = DEPTH, D_MODEL
    nrm = lambda k, shape, s: jax.random.normal(k, shape, f32) * s
    return {
        "x": nrm(ks[0], (BATCH, SEQ, D), 1.0),
        "c": nrm(ks[1], (BATCH, D), 1.0),
        "ada_w": nrm(ks[2], (L, D, N_MOD * D), 0.5 * D ** -0.5),
        "ada_b": nrm(ks[3], (L, N_MOD * D), 0.02),
        "norm1_g": 1.0 + nrm(ks[4], (L, D), 0.05),
        "w_in": nrm(ks[5], (L, D, D_IN), D ** -0.5),
        "b_in": nrm(ks[6], (L, D_IN), 0.02),
        "conv_w": nrm(ks[7], (L, CONV_KERNEL, D_CONV), CONV_KERNEL ** -0.5),
        "conv_b": nrm(ks[8], (L, D_CONV), 0.02),
        "conv_ln_g": 1.0 + nrm(ks[9], (L, D_CONV), 0.05),
        "conv_ln_b": nrm(ks[10], (L, D_CONV), 0.02),
        "w_conv_out": nrm(ks[11], (L, D_CONV, D), D_CONV ** -0.5),
        "pool_w": nrm(ks[12], (L, N_POOL_GROUPS, POOL_GROUP, POOL_GROUP), POOL_GROUP ** -0.5),
        "pool_scale": 0.5 + nrm(ks[13], (L, D_POOL), 0.1),
        "w_out": nrm(ks[14], (L, D, D), D ** -0.5),
        "b_out": nrm(ks[15], (L, D), 0.02),
        "norm2_g": 1.0 + nrm(ks[16], (L, D), 0.05),
        "peer_wq": nrm(ks[17], (L, D, PEER_HEADS * PEER_DKEY), D ** -0.5),
        "peer_keys": nrm(ks[18], (L, PEER_HEADS, 2, PEER_NKEYS, PEER_DHALF), PEER_DHALF ** -0.5),
        "peer_u": nrm(ks[19], (L, PEER_EXPERTS, D), D ** -0.5),
        "peer_v": nrm(ks[20], (L, PEER_EXPERTS, D), 1.0),
        "final_g": 1.0 + nrm(ks[21], (D,), 0.05),
    }

def reference(x, c, ada_w, ada_b, norm1_g, w_in, b_in, conv_w, conv_b, conv_ln_g, conv_ln_b,
              w_conv_out, pool_w, pool_scale, w_out, b_out, norm2_g, peer_wq, peer_keys,
              peer_u, peer_v, final_g):
    B, S, D = x.shape
    c_act = jax.nn.silu(c)
    for l in range(DEPTH):
        mod = c_act @ ada_w[l] + ada_b[l]
        sh1, sc1, g1, sh2, sc2, g2 = jnp.split(mod, N_MOD, axis=-1)

        h = _modulate(_rmsnorm(x, norm1_g[l]), sh1, sc1)
        z = h @ w_in[l] + b_in[l]
        za, zb, zp, zg = jnp.split(z, [D_CONV, 2 * D_CONV, 2 * D_CONV + D_POOL], axis=-1)
        conv_out = _conv_branch(za, zb, conv_w[l], conv_b[l], conv_ln_g[l], conv_ln_b[l], w_conv_out[l])
        pooled = _causal_pool(zp)
        pool_out = jnp.einsum("bsgc,gcd->bsgd", pooled, pool_w[l]).reshape(B, S, D_POOL) * pool_scale[l]
        gates = jax.nn.sigmoid(zg).reshape(B, S, N_BRANCHES, D)
        y = gates[:, :, 0] * conv_out + gates[:, :, 1] * pool_out
        x = x + g1[:, None, :] * (y @ w_out[l] + b_out[l])

        h = _modulate(_rmsnorm(x, norm2_g[l]), sh2, sc2)
        x = x + g2[:, None, :] * _peer(h, peer_wq[l], peer_keys[l], peer_u[l], peer_v[l])
    return _rmsnorm(x, final_g)


_drawn_inputs = setup_inputs


def setup_inputs(seed=0):
    import zlib

    import numpy as np

    out = dict(_drawn_inputs(seed))
    spreads = {}
    factors = {'b_in': 3.423, 'conv_b': 2.781, 'conv_ln_b': 3.377}
    for name, (base, spread) in spreads.items():
        noise = np.random.default_rng([zlib.crc32(name.encode()), seed]).standard_normal(out[name].shape)
        drawn = base * np.exp(spread * noise) if base else spread * noise
        out[name] = __import__('jax').numpy.asarray(drawn.astype(out[name].dtype))
    for name, factor in factors.items():
        out[name] = (out[name] * factor).astype(out[name].dtype)
    return out
```

```python
import numpy as np
import concourse.bass as bass
from concourse import mybir
from concourse.alu_op_type import AluOpType as ALU
from contextlib import ExitStack

F32 = mybir.dt.float32
F32R = mybir.dt.float32r
U32 = mybir.dt.uint32
ACT = mybir.ActivationFunctionType
AX = mybir.AxisListType

P = 128
D = 1024
T = 256
DEPTH = 2
KD = D // P
TT = T // P
TAPS = 31
PADC = TAPS - 1
WINDOWS = (2, 4, 8, 16)
PADP = 16
HEADS = 8
HP = 2 * HEADS
NKEYS = 128
TOPK = 16
CHUNKS = NKEYS
EPS = 1e-6
NEG = -3.0e38

SLOTS = 4
SLOT = 2048
SEC = 1024
NB = SEC // SLOTS
CPS = 2
CSEC = SLOTS * CPS
USECS = CHUNKS // CSEC

S_ADA, N_ADA = 0, 6
S_IN, N_IN = S_ADA + N_ADA, 5
S_CO = S_IN + N_IN
S_OUT = S_CO + 1
S_Q, N_Q = S_OUT + 1, 2
S_U = S_Q + N_Q
S_V = S_U + USECS
N_SEC = S_V + USECS

V_N1, V_BIN, V_CB, V_LG, V_LB, V_PS, V_BO, V_N2 = 0, 8, 48, 56, 64, 72, 80, 88
ROWS_A = 96
V_ADAB, V_C, V_FG = ROWS_A, ROWS_A + 48, ROWS_A + 56
ROWS_B = 64
NVEC = ROWS_A + ROWS_B
M_SH1, M_SC1, M_G1, M_SH2, M_SC2, M_G2 = (KD * i for i in range(6))

TG = 4
NTG = T // TG


def build(nc, x, c, ada_w, ada_b, norm1_g, w_in, b_in, conv_w, conv_b, conv_ln_g, conv_ln_b, w_conv_out,
          pool_w, pool_scale, w_out, b_out, norm2_g, peer_wq, peer_keys, peer_u, peer_v, final_g, out):
    ctx = ExitStack()
    with ctx:
        def sb(name, shape, dt=F32, stack=ctx):
            return stack.enter_context(nc.sbuf_tensor(name, shape, dt))

        def sem(name):
            return ctx.enter_context(nc.semaphore(name))

        ring = sb("ring", [P, SLOTS, SLOT])
        x_t = sb("x_t", [P, KD, T])
        ident = sb("ident", [P, P])
        mean_w = sb("mean_w", [P, P])
        iota = sb("iota", [P, P])
        vecs = sb("vecs", [P, DEPTH * NVEC])
        lv = sb("lv", [P, NVEC])
        c_act = sb("c_act", [P, KD])
        mod = sb("mod", [P, 6 * KD])
        amp = sb("amp", [P, 2, KD])
        g1b = sb("g1b", [P, KD])
        inv_n = sb("inv_n", [P, PADP])
        eps = sb("eps", [P, 1])
        own_i2 = sb("own_i2", [P, 2 * TG])
        ps = ctx.enter_context(nc.psum_tensor("ps", [P, 8, 512], F32))

        mix = ExitStack()
        h = sb("h", [P, KD, T], stack=mix)
        sq = sb("sq", [P, KD, T], stack=mix)
        scaled = sb("scaled", [P, KD, T], stack=mix)
        u_pad = sb("u_pad", [P, KD, PADC + T], stack=mix)
        conv = sb("conv", [P, KD, T], stack=mix)
        p_pad = sb("p_pad", [P, KD, PADP + T], stack=mix)
        win_a = sb("win_a", [P, KD, PADP + T], stack=mix)
        win_b = sb("win_b", [P, KD, PADP + T], stack=mix)
        gates_q = sb("gates_q", [P, HP, T], stack=mix)
        gate_a, gate_b, q_t = gates_q[:, 0:KD, :], gates_q[:, KD:2 * KD, :], gates_q
        pool_out = sb("pool_out", [P, KD, T], stack=mix)
        val_y = sb("val_y", [P, KD, T], stack=mix)
        keys_n = sb("keys_n", [P, HP, P], stack=mix)
        keys_t = sb("keys_t", [P, HP, P], stack=mix)
        pw = sb("pw", [P, KD, 2 * P], stack=mix)
        cw_n = sb("cw_n", [124, 2, P], stack=mix)
        cw = sb("cw", [P, 2 * 124], stack=mix)
        root = sb("root", [P, T], stack=mix)
        rs = sb("rs", [P, T], stack=mix)
        rows = sb("rows", [P, 2 * DEPTH, P], stack=mix)
        mix.close()
        gs = sb("gs", [P, CHUNKS * T])
        st_hi = sb("st_hi", [P, 2, D], F32R)
        st_lo = sb("st_lo", [P, 2, D], F32R)
        idx_t = sb("idx_t", [P, 3, T])
        part = ExitStack()
        h_hi = sb("h_hi", [P, KD, T], F32R, stack=part)
        h_lo = sb("h_lo", [P, KD, T], F32R, stack=part)
        part.close()
        hot1 = sb("hot1", [P, 2, TG, P])
        hot2 = sb("hot2", [P, 2, TG, P])
        p_hi = sb("p_hi", [P, 2, T], F32R)
        p_lo = sb("p_lo", [P, 2, T], F32R)

        R0 = 96 * T

        def tail(at, n, dt=F32):
            v = gs[:, R0 + at:R0 + at + n]
            return v if dt is F32 else v.bitcast(dt)
        scores = tail(0, TT * HP * P)
        B0 = TT * HP * P
        top_v = tail(B0, 512)
        top_i = tail(B0 + 512, 512)
        logits = tail(B0 + 1024, 256)
        picks = tail(B0 + 1280, 768)
        cand = tail(B0 + 2048, 256)
        cand2 = tail(B0 + 2304, 256)
        pick_hot = tail(B0 + 2560, 256)
        pick_hot2 = tail(B0 + 2816, 256)
        work = tail(B0 + 3072, P)
        work2 = tail(B0 + 3200, P)
        best_v = tail(B0 + 3328, TOPK)
        best_i = tail(B0 + 3344, TOPK, U32)
        pos = tail(B0 + 3360, TOPK, U32)
        pos_f = tail(B0 + 3376, TOPK)
        shifted = tail(B0 + 3392, 256)
        expo = tail(B0 + 3648, 256)
        total = tail(B0 + 3904, TT * HEADS)
        total_r = tail(B0 + 3920, TT * HEADS)
        o_sb = gs[:, 0:TT * D].rearrange("p (a d) -> p a d", a=TT)

        ring_full = [sem(f"ring_full{s}") for s in range(SLOTS)]
        slot_read = [sem(f"slot_read{s}") for s in range(SLOTS)]
        rows_in = sem("rows_in")
        x_in = sem("x_in")
        small_in = sem("small_in")
        out_done = sem("out_done")
        consts_ready = sem("consts_ready")
        start_mm = sem("start_mm")
        vecs_ready = sem("vecs_ready")
        c_ready = sem("c_ready")
        x_ready = sem("x_ready")
        setup_mm = sem("setup_mm")
        setup_ready = sem("setup_ready")
        mod_ready = sem("mod_ready")
        sq_ready = sem("sq_ready")
        mean_mm = sem("mean_mm")
        root_ready = sem("root_ready")
        scaled_ready = sem("scaled_ready")
        h_ready = sem("h_ready")
        h_lo_ready = sem("h_lo_ready")
        z_out = sem("z_out")
        conv_ready = sem("conv_ready")
        cen_mm = sem("cen_mm")
        cen_ready = sem("cen_ready")
        conv_act = sem("conv_act")
        pooled_ready = sem("pooled_ready")
        pool_mm = sem("pool_mm")
        pool_ready = sem("pool_ready")
        y_ready = sem("y_ready")
        res_ready = sem("res_ready")
        q_out = sem("q_out")
        score_mm = sem("score_mm")
        score_a = sem("score_a")
        score_v = sem("score_v")
        ut_mm = sem("ut_mm")
        ut_hi = sem("ut_hi")
        ut_lo = sem("ut_lo")
        s_mm = sem("s_mm")
        s_act = sem("s_act")
        logits_ready = sem("logits_ready")
        expo_ready = sem("expo_ready")
        picks_ready = sem("picks_ready")
        picks_mm = sem("picks_mm")
        idx_ready = sem("idx_ready")
        hot1_ready = sem("hot1_ready")
        hot2_ready = sem("hot2_ready")
        w_mm = sem("w_mm")
        w_used = sem("w_used")
        v_hi_ready = sem("v_hi_ready")
        v_lo_ready = sem("v_lo_ready")
        pv_mm = sem("pv_mm")
        o_a = sem("o_a")
        o_v = sem("o_v")
        o_mm = sem("o_mm")
        fin_ready = sem("fin_ready")

        def kview(w):
            return w.rearrange("l (k p) n -> l p k n", p=P)
        ada_v, in_v, co_v, wo_v, wq_v = (kview(w) for w in (ada_w, w_in, w_conv_out, w_out, peer_wq))
        u_v, v_v = (w.rearrange("l (c p) d -> l p c d", p=P) for w in (peer_u, peer_v))
        cw_v = conv_w.rearrange("l k (g p) -> l (k g) p", p=P)
        keys_v = peer_keys.rearrange("l h a n k -> l n (h a) k")
        pw_v = pool_w.rearrange("l g (k p) d -> l p (g k) d", p=P)

        def slot_done(eng, s, l, section, i=0):
            eng.wait_ge(slot_read[s], (l * N_SEC + i) + (section + 2))

        passed = sem("passed")

        def wait_alone(eng, semaphore, value):
            eng.wait_ge(semaphore, value)
            eng.sem_inc(passed, 1)

        block = ctx.enter_context(nc.Block())

        @block.sync
        def _(sp):
            sp.dma_start(val_y[:, :, :].rearrange("p (a k) t -> p a (k t)", a=TT),
                         x[0].rearrange("(a p) d -> p a d", p=P)).then_inc(x_in, 16)

            def stream(l, first, count, source):
                with sp.Fori(0, count) as i:
                    for s in range(SLOTS):
                        sp.wait_ge(slot_read[s], (l * N_SEC + i) + (first + 1))
                        dst, src = source(i, s)
                        sp.dma_start(dst, src).then_inc(ring_full[s], 16)

            def columns(l, w):
                return lambda i, s: (ring[:, s, :].rearrange("p (k n) -> p k n", k=KD),
                                     w[l, :, :, bass.ds(i * SEC + s * NB, NB)])

            def experts(l, w):
                return lambda i, s: (ring[:, s, :].rearrange("p (c d) -> p c d", c=CPS),
                                     w[l, :, bass.ds(i * CSEC + s * CPS, CPS), :])

            with sp.Fori(0, DEPTH) as l:
                stream(l, S_ADA, N_ADA, columns(l, ada_v))
                stream(l, S_IN, N_IN, columns(l, in_v))
                stream(l, S_CO, 1, columns(l, co_v))
                stream(l, S_OUT, 1, columns(l, wo_v))
                stream(l, S_Q, N_Q, columns(l, wq_v))
                stream(l, S_U, USECS, experts(l, u_v))
                stream(l, S_V, USECS, experts(l, v_v))
            sp.wait_ge(fin_ready, 2)
            sp.dma_start(out[0].rearrange("(a p) d -> p a d", p=P), o_sb).then_inc(out_done, 16)
            sp.wait_ge(out_done, 16)

        @block.gpsimd
        def _(pool):
            pool.memset(ident[:, :], 0.0)
            pool.memset(mean_w[:, :], 1.0 / D)
            pool.memset(eps[:, :], EPS)
            for t in range(PADP):
                pool.memset(inv_n[:, t:t + 1], 1.0 / (t + 1))
            pool.iota(iota[:, :], pattern=[[1, P]], base=0, channel_multiplier=0,
                      allow_small_or_imprecise_dtypes=True)
            pool.drain()
            pool.affine_select(out=ident[:, :], in_=ident[:, :], compare_op=ALU.not_equal, fill=1.0,
                               base=0, pattern=[[-1, P]], channel_multiplier=1).then_inc(consts_ready, 1)

            with pool.Fori(0, DEPTH) as l:
                wait_alone(pool, x_ready, l * 2 + 1)
                pool.memset(p_pad[:, :, 0:PADP], 0.0)
                wait_alone(pool, z_out, l * (N_IN * KD) + (KD + 3 * KD))
                pool.drain()

                def window(dst, src, g, lo, shift):
                    k = 2 * g
                    end = PADP + T
                    pool.tensor_tensor(dst[:, k:KD, lo:end], src[:, k:KD, lo:end],
                                       src[:, k:KD, lo - shift:end - shift], ALU.add)
                    pool.drain()
                window(win_a, p_pad, 0, 1, 1)
                window(win_b, win_a, 1, 3, 2)
                window(win_a, win_b, 2, 7, 4)
                window(win_b, win_a, 3, 15, 8)
                for g, w in enumerate(WINDOWS):
                    v = (win_a, win_b)[g % 2][:, 2 * g:2 * g + 2, PADP:PADP + T]
                    pool.tensor_scalar(v[:, :, w - 1:T], v[:, :, w - 1:T], 1.0 / w, None, ALU.mult)
                    pool.tensor_tensor(v[:, :, 0:w - 1], v[:, :, 0:w - 1],
                                       inv_n[:, 0:w - 1].unsqueeze(1).broadcast_to([P, 2, w - 1]), ALU.mult)
                pool.drain()
                for g, w in enumerate(WINDOWS):
                    v = (win_a, win_b)[g % 2][:, 2 * g:2 * g + 2, PADP:PADP + T]
                    last = pool.tensor_tensor(v, v,
                                              p_pad[:, 2 * g:2 * g + 2, PADP:PADP + T], ALU.subtract)
                last.then_inc(pooled_ready, 1)

                pool.wait_ge(idx_ready, l + 1)
                wait_alone(pool, s_mm, l * CHUNKS + (CHUNKS + 2))
                with pool.Fori(0, NTG // 2) as i:
                    pool.drain()
                    pool.tensor_copy(own_i2[:, :], idx_t[:, 1, bass.ds(i * (2 * TG), 2 * TG)])
                    pool.drain()
                    for b in range(2):
                        wait_alone(pool, w_mm, (l * NTG + i * 2) + (b + 1))
                        for k in range(TG):
                            last = pool.tensor_scalar(hot2[:, b, k, :], iota[:, :],
                                                      own_i2[:, b * TG + k:b * TG + k + 1], None, ALU.is_equal)
                        last.then_inc(hot2_ready, 1)

        @block.scalar
        def _(act):
            for l in range(DEPTH):
                at = 0
                for w, n in ((norm1_g, 8), (b_in, 40), (conv_b, 8), (conv_ln_g, 8), (conv_ln_b, 8),
                             (pool_scale, 8), (b_out, 8), (norm2_g, 8)):
                    act.dma_start(rows[at:at + n, 2 * l, :], w[l].rearrange("(r p) -> r p", p=P)).then_inc(rows_in, 16)
                    at += n
                act.dma_start(rows[0:48, 2 * l + 1, :], ada_b[l].rearrange("(r p) -> r p", p=P)).then_inc(rows_in, 16)
                act.dma_start(rows[48:56, 2 * l + 1, :], c[0].rearrange("(r p) -> r p", p=P)).then_inc(rows_in, 16)
                act.dma_start(rows[56:64, 2 * l + 1, :], final_g.rearrange("(r p) -> r p", p=P)).then_inc(rows_in, 16)
            act.sem_inc(z_out, KD)
            act.sem_inc(q_out, KD)
            act.sem_inc(s_act, 2)
            act.sem_inc(ut_hi, 2)
            act.wait_ge(vecs_ready, 1)
            act.activation(c_act[:, :], vecs[:, V_C:V_C + KD], ACT.Silu).then_inc(c_ready, 1)

            def norm_root(l, n, per):
                act.activation(sq[:, :, :], x_t[:, :, :], ACT.Square).then_inc(sq_ready, 1)
                act.wait_ge(mean_mm, l * per + n)
                act.activation(root[:, :], ps[:, 6, 0:T], ACT.Sqrt, bias=eps[:, 0:1]).then_inc(root_ready, 1)

            with act.Fori(0, DEPTH) as l:
                act.wait_ge(x_ready, l * 2 + 1)
                for i in range(2):
                    act.dma_start(cw_n[:, i, :], cw_v[l, 124 * i:124 * i + 124, :]).then_inc(small_in, 16)
                for i in range(2):
                    act.dma_start(keys_n[:, KD * i:KD * (i + 1), :],
                                  keys_v[l, :, KD * i:KD * (i + 1), :]).then_inc(small_in, 16)
                act.dma_start(pw[:, :, :], pw_v[l]).then_inc(small_in, 16)
                norm_root(l, 1, 3)
                act.wait_ge(mod_ready, l + 1)
                for k in range(KD):
                    act.wait_ge(scaled_ready, l * (3 * KD) + (k + 1))
                    act.activation(h[:, k, :], scaled[:, k, :], ACT.Identity,
                                   bias=mod[:, M_SH1 + k:M_SH1 + k + 1]).then_inc(h_ready, 1)
                for i, (dst, func) in enumerate(((val_y, ACT.Identity), (sq, ACT.Sigmoid), (p_pad, ACT.Identity),
                                                 (gate_a, ACT.Sigmoid), (gate_b, ACT.Sigmoid))):
                    for j in range(KD):
                        if j % 2 == 0:
                            slot_done(act, j // 2, l, S_IN + i)
                        o = dst[:, j, PADP:PADP + T] if i == 2 else dst[:, j, :]
                        act.activation(o, ps[:, j, 0:T], func,
                                       bias=lv[:, V_BIN + i * KD + j:V_BIN + i * KD + j + 1]).then_inc(z_out, 1)
                act.wait_ge(cen_ready, l + 1)
                act.activation(sq[:, :, :], conv[:, :, :], ACT.Square).then_inc(sq_ready, 1)
                act.wait_ge(mean_mm, l * 3 + 2)
                act.activation(root[:, :], ps[:, 6, 0:T], ACT.Sqrt, bias=eps[:, 0:1]).then_inc(root_ready, 1)
                for k in range(KD):
                    act.wait_ge(scaled_ready, l * (3 * KD) + (KD + k + 1))
                    act.activation(conv[:, k, :], scaled[:, k, :], ACT.Silu, bias=lv[:, V_LB + k:V_LB + k + 1],
                                   scale=lv[:, V_LG + k:V_LG + k + 1]).then_inc(conv_act, 1)
                for j in range(KD):
                    if j % 2 == 0:
                        slot_done(act, j // 2, l, S_OUT)
                    act.activation(scaled[:, j, :], ps[:, j, 0:T], ACT.Identity, bias=g1b[:, j:j + 1],
                                   scale=mod[:, M_G1 + j:M_G1 + j + 1]).then_inc(res_ready, 1)
                act.wait_ge(x_ready, l * 2 + 2)
                norm_root(l, 3, 3)
                for k in range(KD):
                    act.wait_ge(scaled_ready, l * (3 * KD) + (2 * KD + k + 1))
                    act.activation(h[:, k, :], scaled[:, k, :], ACT.Identity, bias=mod[:, M_SH2 + k:M_SH2 + k + 1])
                    act.activation(h_hi[:, k, :], scaled[:, k, :], ACT.Identity,
                                   bias=mod[:, M_SH2 + k:M_SH2 + k + 1]).then_inc(h_ready, 1)
                for j in range(HP):
                    if j % 2 == 0:
                        slot_done(act, j % KD // 2, l, S_Q + j // KD)
                    act.activation(q_t[:, j, :], ps[:, j % KD, 0:T], ACT.Copy).then_inc(q_out, 1)
                act.wait_ge(score_mm, l * TT + 2)
                act.activation(scores[:, HP * P:2 * HP * P].rearrange("p (b n) -> p b n", n=512),
                               ps[:, 4:8, :], ACT.Copy).then_inc(score_a, 1)

                def round_u(sec, n):
                    sec, n = sec + n // CSEC, n % CSEC
                    cc, b = sec * CSEC + n, n % 2
                    if b == 0:
                        act.wait_ge(ut_mm, (l * (CHUNKS // 2) + sec * (CSEC // 2)) + (n // 2 + 1))
                    else:
                        slot_done(act, n // CPS, l, S_U, sec)
                    act.wait_ge(s_mm, (l * CHUNKS + cc) + 1)
                    act.activation(st_hi[:, b, :].rearrange("p (a n) -> p a n", a=2),
                                   ps[:, 2 * b:2 * b + 2, :], ACT.Copy).then_inc(ut_hi, 1)

                def gelu(cc, b):
                    act.wait_ge(s_mm, (l * CHUNKS + cc) + 3)
                    act.activation(gs[:, bass.ds(cc * T, T)], ps[:, 4 + b, 0:T], ACT.Gelu).then_inc(s_act, 1)

                def u_section(i, last=False):
                    for n in range(CSEC):
                        if not (last and n == CSEC - 1):
                            round_u(i, n + 1)
                        gelu(i * CSEC + n, n % 2)

                round_u(0, 0)
                with act.Fori(0, 10) as i:
                    u_section(i)
                act.wait_ge(logits_ready, l + 1)
                act.activation(expo, shifted, ACT.Exp).then_inc(expo_ready, 1)
                with act.Fori(10, USECS - 1) as i:
                    u_section(i)
                u_section(USECS - 1, last=True)

                act.wait_ge(w_used, l * NTG + (NTG + 2))
                with act.Fori(0, USECS) as i:
                    for n in range(CSEC):
                        b = n % 2
                        if n % CPS == 0:
                            act.wait_ge(ring_full[n // CPS], (l * N_SEC + i) * 16 + (S_V + 1) * 16)
                        act.wait_ge(pv_mm, (l * CHUNKS + i * CSEC) + (n + 1))
                        act.activation(st_hi[:, b, :], ring[:, n // CPS, b * D:(b + 1) * D], ACT.Copy)
                        act.activation(p_hi[:, b, :], gs[:, bass.ds(i * (CSEC * T) + n * T, T)],
                                       ACT.Copy).then_inc(v_hi_ready, 1)
                act.wait_ge(pv_mm, l * CHUNKS + (CHUNKS + 2))
                act.activation(o_sb[:, 0, :].rearrange("p (a n) -> p a n", a=2), ps[:, 0:2, :], ACT.Copy).then_inc(o_a, 1)

            act.wait_ge(x_ready, 2 * DEPTH + 1)
            norm_root(0, 3 * DEPTH + 1, 0)
            act.wait_ge(o_mm, DEPTH + 1)
            act.activation(o_sb[:, 0, :].rearrange("p (a n) -> p a n", a=2), ps[:, 0:2, :], ACT.Copy).then_inc(fin_ready, 1)

        @block.vector
        def _(dve):
            dve.sem_inc(ut_lo, 2)
            dve.sem_inc(w_used, 2)
            dve.wait_ge(start_mm, 1)
            for l in range(DEPTH):
                dve.tensor_copy(vecs[:, l * NVEC:l * NVEC + ROWS_A], ps[:, 2 * l, 0:ROWS_A])
                last = dve.tensor_copy(vecs[:, l * NVEC + ROWS_A:(l + 1) * NVEC], ps[:, 2 * l + 1, 0:ROWS_B])
            last.then_inc(vecs_ready, 1)
            dve.wait_ge(start_mm, 2)
            dve.tensor_copy(x_t[:, :, :].rearrange("p (b c) t -> p b (c t)", c=2), ps[:, 4:8, :]).then_inc(x_ready, 1)

            def norm_scale(l, n, gain):
                dve.wait_ge(root_ready, n)
                dve.reciprocal(rs[:, :], root[:, :])
                dve.drain()
                for k in range(KD):
                    dve.scalar_tensor_tensor(scaled[:, k, :], x_t[:, k, :], gain(k), rs[:, :], ALU.mult,
                                             ALU.mult).then_inc(scaled_ready, 1)

            with dve.Fori(0, DEPTH) as l:
                dve.wait_ge(x_ready, l * 2 + 1)
                dve.tensor_copy(lv[:, :], vecs[:, bass.ds(l * NVEC, NVEC)])
                dve.memset(u_pad[:, :, 0:PADC], 0.0)
                dve.wait_ge(setup_mm, l + 1)
                dve.tensor_copy(keys_t[:, :, :].rearrange("p (b c) n -> p b (c n)", c=4), ps[:, 0:4, :])
                dve.tensor_copy(cw[:, :], ps[:, 4, 0:2 * 124]).then_inc(setup_ready, 1)
                dve.drain()
                slot_done(dve, SLOTS - 1, l, S_ADA + N_ADA - 1)
                dve.tensor_tensor(mod[:, :], ps[:, 5, 0:6 * KD], lv[:, V_ADAB:V_ADAB + 6 * KD], ALU.add)
                dve.drain()
                for n, (sc, g) in enumerate(((M_SC1, V_N1), (M_SC2, V_N2))):
                    dve.scalar_tensor_tensor(amp[:, n, :], mod[:, sc:sc + KD], 1.0, lv[:, g:g + KD], ALU.add, ALU.mult)
                dve.tensor_tensor(g1b[:, :], mod[:, M_G1:M_G1 + KD], lv[:, V_BO:V_BO + KD], ALU.mult).then_inc(mod_ready, 1)
                dve.drain()
                norm_scale(l, l * 3 + 1, lambda k: amp[:, 0, k:k + 1])
                for j in range(KD):
                    dve.wait_ge(z_out, l * (N_IN * KD) + (KD + KD + j + 1))
                    dve.tensor_tensor(u_pad[:, j, PADC:PADC + T], val_y[:, j, :], sq[:, j, :], ALU.mult)
                dve.drain()
                for k in range(KD):
                    dve.tensor_scalar(conv[:, k, :], u_pad[:, k, 0:T], cw[:, k:k + 1],
                                      lv[:, V_CB + k:V_CB + k + 1], ALU.mult, ALU.add)
                with dve.Fori(1, TAPS) as tap:
                    dve.drain()
                    for k in range(KD):
                        dve.scalar_tensor_tensor(conv[:, k, :], u_pad[:, k, bass.ds(tap, T)],
                                                 cw[:, bass.ds(tap * KD + k, 1)], conv[:, k, :], ALU.mult, ALU.add)
                dve.drain().then_inc(conv_ready, 1)
                dve.wait_ge(cen_mm, l + 1)
                dve.tensor_tensor(conv[:, :, :], conv[:, :, :], ps[:, 7, 0:T].unsqueeze(1).broadcast_to([P, KD, T]),
                                  ALU.subtract).then_inc(cen_ready, 1)
                for j in range(KD):
                    dve.wait_ge(pool_mm, l * KD + (j + 1))
                    dve.scalar_tensor_tensor(pool_out[:, j, :], ps[:, j // 2, (j % 2) * T:(j % 2 + 1) * T],
                                             lv[:, V_PS + j:V_PS + j + 1], gate_b[:, j, :], ALU.mult,
                                             ALU.mult).then_inc(pool_ready, 1)
                dve.wait_ge(root_ready, l * 3 + 2)
                dve.reciprocal(rs[:, :], root[:, :])
                dve.drain()
                for k in range(KD):
                    dve.tensor_tensor(scaled[:, k, :], conv[:, k, :], rs[:, :], ALU.mult).then_inc(scaled_ready, 1)
                for j in range(KD):
                    if j % 2 == 0:
                        slot_done(dve, j // 2, l, S_CO)
                    dve.tensor_tensor(val_y[:, j, :], ps[:, j, 0:T], gate_a[:, j, :], ALU.mult)
                dve.drain()
                dve.tensor_tensor(val_y[:, :, :], val_y[:, :, :], pool_out[:, :, :], ALU.add).then_inc(y_ready, 1)
                for j in range(KD):
                    dve.wait_ge(res_ready, l * KD + (j + 1))
                    last = dve.tensor_tensor(x_t[:, j, :], x_t[:, j, :], scaled[:, j, :], ALU.add)
                last.then_inc(x_ready, 1)
                norm_scale(l, l * 3 + 3, lambda k: amp[:, 1, k:k + 1])
                for k in range(KD):
                    dve.wait_ge(h_ready, l * (2 * KD) + (KD + k + 1))
                    last = dve.tensor_tensor(h_lo[:, k, :], h[:, k, :], h_hi[:, k, :].bitcast(F32), ALU.subtract)
                last.then_inc(h_lo_ready, 1)
                dve.wait_ge(score_mm, l * TT + 1)
                dve.tensor_copy(scores[:, 0:HP * P].rearrange("p (b n) -> p b n", n=512), ps[:, 0:4, :]).then_inc(score_v, 1)
                wait_alone(dve, score_a, l + 1)

                def rest_u(cc, b):
                    dve.wait_ge(ut_hi, (l * CHUNKS + cc) + 3)
                    dve.tensor_tensor(st_lo[:, b, :].rearrange("p (a n) -> p a n", a=2), ps[:, 2 * b:2 * b + 2, :],
                                      st_hi[:, b, :].bitcast(F32).rearrange("p (a n) -> p a n", a=2),
                                      ALU.subtract).then_inc(ut_lo, 1)

                def top16(values, spare, n_idx):
                    dve.max(best_v[:, 0:8], values)
                    dve.drain()
                    dve.match_replace(out=spare, in_to_replace=best_v[:, 0:8], in_values=values, imm_value=NEG)
                    dve.max_index(n_idx[:, 0:8], best_v[:, 0:8], values)
                    dve.drain()
                    dve.max(best_v[:, 8:16], spare)
                    dve.drain()
                    dve.max_index(n_idx[:, 8:16], best_v[:, 8:16], spare)
                    dve.drain()

                with dve.Fori(0, 4) as i:
                    for n in range(CSEC):
                        rest_u(i * CSEC + n, n % 2)
                        dve.tensor_copy(work, scores[:, bass.ds(i * (CSEC * P) + n * P, P)])
                        dve.drain()
                        top16(work, work2, best_i)
                        dve.tensor_copy(top_v[:, bass.ds(i * (CSEC * TOPK) + n * TOPK, TOPK)], best_v)
                        dve.tensor_copy(top_i[:, bass.ds(i * (CSEC * TOPK) + n * TOPK, TOPK)], best_i)
                dve.drain()
                with dve.Fori(0, 4) as i:
                    for n in range(CSEC):
                        rest_u((i * CSEC + 4 * CSEC) + n, n % 2)
                        at = i * (CSEC * TOPK) + (n // 2) * 2 * TOPK
                        th = i * (CSEC // 2 * TOPK) + (n // 2) * TOPK
                        if n % 2 == 0:
                            dve.tensor_tensor(
                                cand.rearrange("p (i j) -> p i j", i=TOPK),
                                top_v[:, bass.ds(at, TOPK)].unsqueeze(2).broadcast_to([P, TOPK, TOPK]),
                                top_v[:, bass.ds(at + TOPK, TOPK)].unsqueeze(1).broadcast_to([P, TOPK, TOPK]), ALU.add)
                            dve.drain()
                            top16(cand, cand2, best_i)
                            dve.tensor_copy(logits[:, bass.ds(th, TOPK)], best_v)
                        else:
                            for half, (a, op) in enumerate(((4, ALU.logical_shift_right), (TOPK - 1, ALU.bitwise_and))):
                                dve.tensor_scalar(pos, best_i, a, None, op)
                                dve.drain()
                                dve.tensor_copy(pos_f, pos)
                                dve.drain()
                                hot = pick_hot.rearrange("p (k j) -> p k j", k=TOPK)
                                hot_b = pick_hot2.rearrange("p (k j) -> p k j", k=TOPK)
                                dve.tensor_tensor(hot, pos_f.unsqueeze(2).broadcast_to([P, TOPK, TOPK]),
                                                  iota[:, 0:TOPK].unsqueeze(1).broadcast_to([P, TOPK, TOPK]), ALU.is_equal)
                                dve.drain()
                                dve.tensor_tensor(hot_b, hot, top_i[:, bass.ds(at + half * TOPK, TOPK)].unsqueeze(1)
                                                  .broadcast_to([P, TOPK, TOPK]), ALU.mult)
                                dve.drain()
                                dve.tensor_reduce(picks[:, bass.ds(th + half * T, TOPK)], hot_b, axis=AX.X, op=ALU.add)
                dve.drain()
                by_head = dict(k=TOPK)
                dve.tensor_tensor(shifted.rearrange("p (g k) -> p g k", **by_head),
                                  logits.rearrange("p (g k) -> p g k", **by_head),
                                  logits.rearrange("p (g k) -> p g k", **by_head)[:, :, 0:1].broadcast_to(
                                      [P, TT * HEADS, TOPK]), ALU.subtract).then_inc(logits_ready, 1)
                with dve.Fori(8, 10) as i:
                    for n in range(CSEC):
                        rest_u(i * CSEC + n, n % 2)
                rest_u(10 * CSEC, 0)
                dve.wait_ge(expo_ready, l + 1)
                dve.tensor_reduce(total, expo.rearrange("p (g k) -> p g k", **by_head), axis=AX.X, op=ALU.add)
                dve.drain()
                dve.reciprocal(total_r, total)
                dve.drain()
                dve.tensor_tensor(picks[:, 2 * T:3 * T].rearrange("p (g k) -> p g k", **by_head),
                                  expo.rearrange("p (g k) -> p g k", **by_head),
                                  total_r.unsqueeze(2).broadcast_to([P, TT * HEADS, TOPK]), ALU.mult).then_inc(picks_ready, 1)
                for n in range(1, CSEC):
                    rest_u(10 * CSEC + n, n % 2)
                for n in range(CSEC):
                    rest_u(11 * CSEC + n, n % 2)
                dve.wait_ge(picks_mm, l + 1)
                dve.tensor_copy(idx_t[:, 0:2, :], ps[:, 6, :].rearrange("p (a t) -> p a t", a=2))
                dve.tensor_copy(idx_t[:, 2, :], ps[:, 7, 0:T]).then_inc(idx_ready, 1)
                with dve.Fori(12, USECS) as i:
                    for n in range(CSEC):
                        rest_u(i * CSEC + n, n % 2)

                def hot_rows(g, b):
                    for k in range(TG):
                        t = g * TG + k
                        last = dve.tensor_scalar(hot1[:, b, k, :], iota[:, :], idx_t[:, 0, bass.ds(t, 1)],
                                                 idx_t[:, 2, bass.ds(t, 1)], ALU.is_equal, ALU.mult)
                    last.then_inc(hot1_ready, 1)

                def weigh(g, b):
                    dve.wait_ge(w_mm, (l * NTG + g) + 3)
                    acts = gs[:, :].rearrange("p (c t) -> p t c", t=T)[:, bass.ds(g * TG, TG), :]
                    dve.tensor_tensor(acts, acts, ps[:, b, :].rearrange("p (t c) -> p t c", t=TG),
                                      ALU.mult).then_inc(w_used, 1)

                dve.wait_ge(s_act, l * CHUNKS + (CHUNKS + 2))
                hot_rows(0, 0)
                hot_rows(1, 1)
                with dve.Fori(0, NTG // 2 - 1) as i:
                    for b in range(2):
                        weigh(i * 2 + b, b)
                        hot_rows(i * 2 + (b + 2), b)
                for b in range(2):
                    weigh(NTG - 2 + b, b)
                dve.drain()

                with dve.Fori(0, USECS) as i:
                    for n in range(CSEC):
                        b = n % 2
                        dve.wait_ge(v_hi_ready, (l * CHUNKS + i * CSEC) + (n + 1))
                        v = dve.tensor_tensor(st_lo[:, b, :], ring[:, n // CPS, b * D:(b + 1) * D],
                                              st_hi[:, b, :].bitcast(F32), ALU.subtract)
                        if b == CPS - 1:
                            v.then_inc(slot_read[n // CPS], 1)
                        dve.tensor_tensor(p_lo[:, b, :], gs[:, bass.ds(i * (CSEC * T) + n * T, T)],
                                          p_hi[:, b, :].bitcast(F32), ALU.subtract).then_inc(v_lo_ready, 1)
                dve.wait_ge(pv_mm, l * CHUNKS + (CHUNKS + 2))
                dve.tensor_copy(o_sb[:, 1, :].rearrange("p (a n) -> p a n", a=2), ps[:, 2:4, :]).then_inc(o_v, 1)
                dve.wait_ge(o_mm, l + 1)
                for k in range(KD):
                    last = dve.scalar_tensor_tensor(x_t[:, k, :], ps[:, 4 + k // 2, (k % 2) * T:(k % 2 + 1) * T],
                                                    mod[:, M_G2 + k:M_G2 + k + 1], x_t[:, k, :], ALU.mult, ALU.add)
                last.then_inc(x_ready, 1)

            norm_scale(0, 3 * DEPTH + 1, lambda k: vecs[:, V_FG + k:V_FG + k + 1])
            dve.wait_ge(o_mm, DEPTH + 1)
            dve.tensor_copy(o_sb[:, 1, :].rearrange("p (a n) -> p a n", a=2), ps[:, 2:4, :]).then_inc(fin_ready, 1)

        @block.tensor
        def _(pe):
            for s in range(SLOTS):
                pe.sem_inc(slot_read[s], 1)
            pe.sem_inc(s_mm, 2)
            pe.sem_inc(w_mm, 2)
            pe.sem_inc(pv_mm, 2)
            pe.wait_ge(consts_ready, 1)
            pe.wait_ge(rows_in, 16 * 11 * DEPTH)
            for l in range(DEPTH):
                pe.transpose(ps[:, 2 * l, 0:ROWS_A], rows[0:ROWS_A, 2 * l, :], ident[0:ROWS_A, 0:ROWS_A])
                last = pe.transpose(ps[:, 2 * l + 1, 0:ROWS_B], rows[0:ROWS_B, 2 * l + 1, :], ident[0:ROWS_B, 0:ROWS_B])
            last.then_inc(start_mm, 1)
            pe.wait_ge(x_in, 16)
            xin = val_y[:, :, :].rearrange("p (a k) t -> p a (k t)", a=TT)

            def to_channels(src):
                for k in range(KD):
                    for a in range(TT):
                        last = pe.transpose(ps[:, 4 + k // 2, (k % 2) * T + a * P:(k % 2) * T + (a + 1) * P],
                                            src[:, a, k * P:(k + 1) * P], ident[:, :])
                return last
            to_channels(xin).then_inc(start_mm, 1)
            pe.wait_ge(c_ready, 1)

            def mean_of(src, bank):
                for k in range(KD):
                    last = pe.matmul(ps[:, bank, 0:T], mean_w[:, :], src[:, k, :], start=(k == 0), stop=(k == KD - 1))
                return last

            def section(l, first, i, src, before=None):
                for j in range(KD):
                    s, half = j // 2, j % 2
                    if half == 0:
                        pe.wait_ge(ring_full[s], (l * N_SEC + i) * 16 + (first + 1) * 16)
                    if before:
                        before(j)
                    for k in range(KD):
                        last = pe.matmul(ps[:, j, 0:T], ring[:, s, k * NB + half * P:k * NB + (half + 1) * P],
                                         src[:, k, :], start=(k == 0), stop=(k == KD - 1))
                    if half:
                        last.then_inc(slot_read[s], 1)

            with pe.Fori(0, DEPTH) as l:
                pe.wait_ge(x_ready, l * 2 + 1)
                pe.wait_ge(small_in, l * (5 * 16) + 5 * 16)
                for j in range(HP):
                    pe.transpose(ps[:, j // 4, (j % 4) * P:(j % 4 + 1) * P], keys_n[:, j, :], ident[:, :])
                for i in range(2):
                    last = pe.transpose(ps[:, 4, i * 124:(i + 1) * 124], cw_n[:, i, :], ident[0:124, 0:124])
                last.then_inc(setup_mm, 1)
                pe.wait_ge(sq_ready, l * 3 + 1)
                mean_of(sq, 6).then_inc(mean_mm, 1)
                with pe.Fori(0, N_ADA) as i:
                    for j in range(KD):
                        s, half = j // 2, j % 2
                        if half == 0:
                            pe.wait_ge(ring_full[s], (l * N_SEC + i) * 16 + (S_ADA + 1) * 16)
                        for k in range(KD):
                            last = pe.matmul(ps[:, 5, bass.ds(i * KD + j, 1)],
                                             ring[:, s, k * NB + half * P:k * NB + (half + 1) * P],
                                             c_act[:, k:k + 1], start=(k == 0), stop=(k == KD - 1))
                        if half:
                            last.then_inc(slot_read[s], 1)
                pe.wait_ge(setup_ready, l + 1)
                wait_alone(pe, h_ready, l * (2 * KD) + KD)
                with pe.Fori(0, N_IN) as i:
                    section(l, S_IN, i, h,
                            lambda j: pe.wait_ge(z_out, (l * (N_IN * KD) + i * KD) + (j + 1)))
                pe.wait_ge(pooled_ready, l + 1)
                pe.wait_ge(z_out, l * (N_IN * KD) + (N_IN * KD + KD))
                for j in range(KD):
                    g, half = j // 2, j % 2
                    for k in range(2):
                        last = pe.matmul(ps[:, j // 2, half * T:(half + 1) * T],
                                         pw[:, 2 * g + k, half * P:(half + 1) * P],
                                         (win_a, win_b)[g % 2][:, 2 * g + k, PADP:PADP + T],
                                         start=(k == 0), stop=(k == 1))
                    last.then_inc(pool_mm, 1)
                pe.wait_ge(conv_ready, l + 1)
                mean_of(conv, 7).then_inc(cen_mm, 1)
                pe.wait_ge(sq_ready, l * 3 + 2)
                mean_of(sq, 6).then_inc(mean_mm, 1)
                pe.wait_ge(pool_ready, l * KD + KD)
                pe.wait_ge(conv_act, l * KD + KD)
                section(l, S_CO, 0, conv)
                pe.wait_ge(y_ready, l + 1)
                section(l, S_OUT, 0, val_y)
                pe.wait_ge(sq_ready, l * 3 + 3)
                mean_of(sq, 6).then_inc(mean_mm, 1)
                wait_alone(pe, h_ready, l * (2 * KD) + 2 * KD)
                with pe.Fori(0, N_Q) as i:
                    section(l, S_Q, i, h, lambda j: pe.wait_ge(q_out, (l * HP + i * KD) + (j + 1)))
                pe.wait_ge(q_out, l * HP + (HP + KD))
                for a in range(TT):
                    for j in range(HP):
                        last = pe.matmul(ps[:, 4 * a + j // 4, (j % 4) * P:(j % 4 + 1) * P],
                                         q_t[:, j, a * P:(a + 1) * P], keys_t[:, j, :], start=True, stop=True)
                    last.then_inc(score_mm, 1)
                pe.wait_ge(score_v, l + 1)
                pe.wait_ge(score_a, l + 1)
                pe.wait_ge(h_lo_ready, l + 1)

                def turn_u(sec, n):
                    sec, n = sec + n // CSEC, n % CSEC
                    cc, b, s = sec * CSEC + n, n % 2, n // CPS
                    if n % CPS == 0:
                        pe.wait_ge(ring_full[s], (l * N_SEC + sec) * 16 + (S_U + 1) * 16)
                    pe.wait_ge(ut_hi, (l * CHUNKS + cc) + 1)
                    pe.wait_ge(ut_lo, (l * CHUNKS + cc) + 1)
                    for k in range(KD):
                        last = pe.transpose(ps[:, 2 * b + k // 4, (k % 4) * P:(k % 4 + 1) * P],
                                            ring[:, s, b * D + k * P:b * D + (k + 1) * P], ident[:, :])
                    last.then_inc(slot_read[s] if b == CPS - 1 else ut_mm, 1)

                def use_u(sec, n):
                    cc, b = sec * CSEC + n, n % 2
                    o = ps[:, 4 + b, 0:T]
                    pe.wait_ge(s_act, (l * CHUNKS + cc) + 1)
                    pe.wait_ge(ut_hi, (l * CHUNKS + cc) + 3)
                    for k in range(KD):
                        pe.matmul(o, st_hi[:, b, k * P:(k + 1) * P], h_hi[:, k, :], start=(k == 0), stop=False)
                        pe.matmul(o, st_hi[:, b, k * P:(k + 1) * P], h_lo[:, k, :], start=False, stop=False)
                    pe.wait_ge(ut_lo, (l * CHUNKS + cc) + 3)
                    for k in range(KD):
                        last = pe.matmul(o, st_lo[:, b, k * P:(k + 1) * P], h_hi[:, k, :], start=False, stop=(k == KD - 1))
                    last.then_inc(s_mm, 1)

                def u_section(i, last=False):
                    for n in range(CSEC):
                        if not (last and n == CSEC - 1):
                            turn_u(i, n + 1)
                        use_u(i, n)
                turn_u(0, 0)
                with pe.Fori(0, 12) as i:
                    u_section(i)
                pe.wait_ge(picks_ready, l + 1)
                for a in range(3):
                    for t in range(TT):
                        last = pe.transpose(ps[:, 6 + a // 2, (a % 2) * T + t * P:(a % 2) * T + (t + 1) * P],
                                            picks[:, a * T + t * P:a * T + (t + 1) * P], ident[:, :])
                last.then_inc(picks_mm, 1)
                with pe.Fori(12, USECS - 1) as i:
                    u_section(i)
                u_section(USECS - 1, last=True)

                with pe.Fori(0, NTG // 2) as i:
                    for b in range(2):
                        pe.wait_ge(w_used, (l * NTG + i * 2) + (b + 1))
                        pe.wait_ge(hot1_ready, (l * NTG + i * 2) + (b + 1))
                        pe.wait_ge(hot2_ready, (l * NTG + i * 2) + (b + 1))
                        for k in range(TG):
                            last = pe.matmul(ps[:, b, k * P:(k + 1) * P], hot2[:, b, k, :], hot1[:, b, k, :],
                                             start=True, stop=True)
                        last.then_inc(w_mm, 1)

                pe.wait_ge(w_used, l * NTG + (NTG + 2))

                def v_section(i, first=False, final=False):
                    for n in range(CSEC):
                        b = n % 2
                        start, stop = first and n == 0, final and n == CSEC - 1
                        pe.wait_ge(v_hi_ready, (l * CHUNKS + i * CSEC) + (n + 1))
                        for a in range(TT):
                            for hf in range(2):
                                pe.matmul(ps[:, 2 * a + hf, :], p_hi[:, b, a * P:(a + 1) * P],
                                          st_hi[:, b, hf * 512:(hf + 1) * 512], start=start, stop=False)
                        pe.wait_ge(v_lo_ready, (l * CHUNKS + i * CSEC) + (n + 1))
                        for a in range(TT):
                            for hf in range(2):
                                pe.matmul(ps[:, 2 * a + hf, :], p_hi[:, b, a * P:(a + 1) * P],
                                          st_lo[:, b, hf * 512:(hf + 1) * 512], start=False, stop=False)
                            for hf in range(2):
                                last = pe.matmul(ps[:, 2 * a + hf, :], p_lo[:, b, a * P:(a + 1) * P],
                                                 st_hi[:, b, hf * 512:(hf + 1) * 512], start=False, stop=stop)
                        last.then_inc(pv_mm, 1)
                v_section(0, first=True)
                with pe.Fori(1, USECS - 1) as i:
                    v_section(i)
                v_section(USECS - 1, final=True)
                pe.wait_ge(o_a, l + 1)
                pe.wait_ge(o_v, l + 1)
                to_channels(o_sb).then_inc(o_mm, 1)

            pe.wait_ge(sq_ready, 3 * DEPTH + 1)
            mean_of(sq, 6).then_inc(mean_mm, 1)
            for k in range(KD):
                pe.wait_ge(scaled_ready, DEPTH * 3 * KD + k + 1)
                for a in range(TT):
                    last = pe.transpose(ps[:, 2 * a + k // 4, (k % 4) * P:(k % 4 + 1) * P],
                                        scaled[:, k, a * P:(a + 1) * P], ident[:, :])
            last.then_inc(o_mm, 1)


_INS = ["x", "c", "ada_w", "ada_b", "norm1_g", "w_in", "b_in", "conv_w", "conv_b", "conv_ln_g", "conv_ln_b",
        "w_conv_out", "pool_w", "pool_scale", "w_out", "b_out", "norm2_g", "peer_wq", "peer_keys", "peer_u",
        "peer_v", "final_g"]


def kernel(**inputs):
    import concourse.bacc as bacc
    from concourse.bass_utils import run_bass_kernel_spmd

    nc = bacc.Bacc("TRN2", target_bir_lowering=False, num_devices=1)
    arrays, args = {}, []
    for name in _INS:
        a = np.ascontiguousarray(inputs[name])
        arrays[f"in_{name}"] = a
        args.append(nc.dram_tensor(f"in_{name}", a.shape, mybir.dt.from_np(a.dtype), kind="ExternalInput").ap())
    args.append(nc.dram_tensor("out_x", (1, T, D), F32, kind="ExternalOutput").ap())
    build(nc, *args)
    r = run_bass_kernel_spmd(nc, [arrays], core_ids=[0])
    return r.results[0]["out_x"]
```

```python
import numpy as np
import concourse.bass as bass
from concourse import mybir
from concourse.alu_op_type import AluOpType as ALU
from contextlib import ExitStack

F32 = mybir.dt.float32
F32R = mybir.dt.float32r
U32 = mybir.dt.uint32
ACT = mybir.ActivationFunctionType
AX = mybir.AxisListType

P = 128
D = 1024
T = 256
DEPTH = 2
KD = D // P
TT = T // P
TAPS = 31
PADC = TAPS - 1
WINDOWS = (2, 4, 8, 16)
PADP = 16
HEADS = 8
HP = 2 * HEADS
NKEYS = 128
TOPK = 16
CHUNKS = NKEYS
EPS = 1e-6
NEG = -3.0e38

SLOTS = 4
SLOT = 2048
SEC = 1024
NB = SEC // SLOTS
CPS = 2
CSEC = SLOTS * CPS
USECS = CHUNKS // CSEC

N_ADA, N_IN = 6, 5
S_ADA01 = 0
S_X = 2
S_IN2 = 6
S_ADA4 = 9
S_CO = 10
S_OUT = 11
S_Y = 12
S_Q1 = 14
S_U = 15
S_V = S_U + USECS
N_SEC = S_V + USECS

W_IN, W_CO, W_OUT, W_Q, N_W = 0, 16, 24, 32, 48


def place(n):
    if n < W_CO:
        return S_X + n // 4, n % 4 // 2
    if n < W_Q:
        return (S_CO if n < W_OUT else S_OUT), n % 8 // 2
    if n < W_Q + KD:
        return S_Y + (n - W_Q) // 4, n % 4 // 2
    return S_Q1, n % 8 // 2


V_N1, V_BIN, V_CB, V_LG, V_LB, V_PS, V_BO, V_N2 = 0, 8, 48, 56, 64, 72, 80, 88
ROWS_A = 96
V_ADAB, V_C, V_FG = ROWS_A, ROWS_A + 48, ROWS_A + 56
ROWS_B = 64
NVEC = ROWS_A + ROWS_B
M_SH1, M_SC1, M_G1, M_SH2, M_SC2, M_G2 = (KD * i for i in range(6))

TG = 4
NTG = T // TG
TB = 4


def build(nc, x, c, ada_w, ada_b, norm1_g, w_in, b_in, conv_w, conv_b, conv_ln_g, conv_ln_b, w_conv_out,
          pool_w, pool_scale, w_out, b_out, norm2_g, peer_wq, peer_keys, peer_u, peer_v, final_g, out):
    ctx = ExitStack()
    with ctx:
        def sb(name, shape, dt=F32, stack=ctx):
            return stack.enter_context(nc.sbuf_tensor(name, shape, dt))

        def sem(name):
            return ctx.enter_context(nc.semaphore(name))

        ring = sb("ring", [P, SLOTS, SLOT])
        x_t = sb("x_t", [P, KD, T])
        ident = sb("ident", [P, P])
        mean_w = sb("mean_w", [P, P])
        iota = sb("iota", [P, P])
        vecs = sb("vecs", [P, DEPTH * NVEC])
        lv = sb("lv", [P, NVEC])
        st_hi = sb("st_hi", [P, 2, D], F32R)
        st_lo = sb("st_lo", [P, 2, D], F32R)
        c_act = sb("c_act", [P, KD])
        mod = sb("mod", [P, 6 * KD])
        amp = sb("amp", [P, 2, KD])
        g1b = sb("g1b", [P, KD])
        inv_n = sb("inv_n", [P, PADP])
        eps = sb("eps", [P, 1])
        ones = sb("ones", [P, 1])
        own = sb("own", [P, 2, TB * TG])
        ps = ctx.enter_context(nc.psum_tensor("ps", [P, 8, 512], F32))

        def tile(j):
            return ps[:, j % 4, 0:T]

        def pair(j):
            return ps[:, j // 2, (j % 2) * T:(j % 2 + 1) * T]

        def weight_tile(s, j):
            return ring[:, s, :].rearrange("p (k n) -> p k n", k=KD)[:, :, (j % 2) * P:(j % 2 + 1) * P]

        def by_group(v):
            return v.rearrange("p (k n) -> p k n", k=KD)

        mix = ExitStack()
        gates_q = sb("gates_q", [P, HP, T], stack=mix)
        keys_t = sb("keys_t", [P, HP, P], stack=mix)
        h = sb("h", [P, KD, T], stack=mix)
        sq = sb("sq", [P, KD, T], stack=mix)
        scaled = sb("scaled", [P, KD, T], stack=mix)
        u_pad = sb("u_pad", [P, KD, PADC + T], stack=mix)
        conv = sb("conv", [P, KD, T], stack=mix)
        p_pad = sb("p_pad", [P, KD, PADP + T], stack=mix)
        win_a = sb("win_a", [P, KD, PADP + T], stack=mix)
        win_b = sb("win_b", [P, KD, PADP + T], stack=mix)
        gate_a, gate_b, q_t = gates_q[:, 0:KD, :], gates_q[:, KD:2 * KD, :], gates_q
        pool_out = sb("pool_out", [P, KD, T], stack=mix)
        val_y = sb("val_y", [P, KD, T], stack=mix)
        keys_n = scaled[:, :, :].rearrange("p k (a n) -> p (k a) n", a=2)
        ada_acc = pool_out[:, :, :].rearrange("p (b k) t -> p b (k t)", b=2)
        ada_acc2 = u_pad[:, :, :].rearrange("p k t -> p (k t)")[:, 0:2 * SEC].rearrange("p (b n) -> p b n", b=2)
        pw = sb("pw", [P, KD, 2 * P], stack=mix)
        cw_n = sb("cw_n", [124, 2, P], stack=mix)
        cw = sb("cw", [P, 2 * 124], stack=mix)
        root = sb("root", [P, T], stack=mix)
        rs = sb("rs", [P, T], stack=mix)
        rows = sb("rows", [P, 2 * DEPTH, P], stack=mix)
        mix.close()
        gs = sb("gs", [P, CHUNKS * T])
        idx_t = sb("idx_t", [P, 3, T])
        part = ExitStack()
        h_hi = sb("h_hi", [P, KD, T], F32R, stack=part)
        h_lo = sb("h_lo", [P, KD, T], F32R, stack=part)
        part.close()
        hot1 = sb("hot1", [P, 2, TG, P])
        hot2 = sb("hot2", [P, 2, TG, P])
        away = sb("away", [P, 2, TG, P])
        p_hi = sb("p_hi", [P, 2, T], F32R)
        p_lo = sb("p_lo", [P, 2, T], F32R)

        R0 = 96 * T

        def tail(at, n, dt=F32):
            v = gs[:, R0 + at:R0 + at + n]
            return v if dt is F32 else v.bitcast(dt)
        scores = tail(0, TT * HP * P)
        B0 = TT * HP * P
        top_v = tail(B0, 512)
        top_i = tail(B0 + 512, 512)
        logits = tail(B0 + 1024, 256)
        picks = tail(B0 + 1280, 768)
        cand = tail(B0 + 2048, 256)
        cand2 = tail(B0 + 2304, 256)
        pick_hot = tail(B0 + 2560, 256)
        pick_hot2 = tail(B0 + 2816, 256)
        work = tail(B0 + 3072, P)
        work2 = tail(B0 + 3200, P)
        best_v = tail(B0 + 3328, TOPK)
        best_i = tail(B0 + 3344, TOPK, U32)
        pos = tail(B0 + 3360, TOPK, U32)
        pos_f = tail(B0 + 3376, TOPK)
        shifted = tail(B0 + 3392, 256)
        expo = tail(B0 + 3648, 256)
        total = tail(B0 + 3904, TT * HEADS)
        total_r = tail(B0 + 3920, TT * HEADS)
        o_sb = gs[:, 0:TT * D].rearrange("p (a d) -> p a d", a=TT)

        ring_full = [sem(f"ring_full{s}") for s in range(SLOTS)]
        slot_read = [sem(f"slot_read{s}") for s in range(SLOTS)]
        rows_in = sem("rows_in")
        x_in = sem("x_in")
        small_in = sem("small_in")
        out_done = sem("out_done")
        consts_ready = sem("consts_ready")
        start_mm = sem("start_mm")
        vecs_ready = sem("vecs_ready")
        c_ready = sem("c_ready")
        x_ready = sem("x_ready")
        setup_mm = sem("setup_mm")
        setup_ready = sem("setup_ready")
        ada_part = sem("ada_part")
        ada_mm = sem("ada_mm")
        w_hi = sem("w_hi")
        w_lo = sem("w_lo")
        part_mm = sem("part_mm")
        x_hi_ready = sem("x_hi_ready")
        y_out = sem("y_out")
        mod_ready = sem("mod_ready")
        sq_ready = sem("sq_ready")
        mean_mm = sem("mean_mm")
        root_ready = sem("root_ready")
        scaled_ready = sem("scaled_ready")
        h_ready = sem("h_ready")
        x_lo_ready = sem("x_lo_ready")
        z_out = sem("z_out")
        conv_ready = sem("conv_ready")
        cen_mm = sem("cen_mm")
        cen_ready = sem("cen_ready")
        conv_act = sem("conv_act")
        pooled_ready = sem("pooled_ready")
        pool_mm = sem("pool_mm")
        pool_ready = sem("pool_ready")
        y_ready = sem("y_ready")
        res_ready = sem("res_ready")
        q_out = sem("q_out")
        score_mm = sem("score_mm")
        score_a = sem("score_a")
        score_v = sem("score_v")
        ut_mm = sem("ut_mm")
        ut_hi = sem("ut_hi")
        ut_lo = sem("ut_lo")
        s_mm = sem("s_mm")
        s_act = sem("s_act")
        logits_ready = sem("logits_ready")
        expo_ready = sem("expo_ready")
        picks_ready = sem("picks_ready")
        picks_mm = sem("picks_mm")
        idx_ready = sem("idx_ready")
        hot1_ready = sem("hot1_ready")
        away_ready = sem("away_ready")
        hot2_ready = sem("hot2_ready")
        w_mm = sem("w_mm")
        w_used = sem("w_used")
        v_hi_ready = sem("v_hi_ready")
        v_lo_ready = sem("v_lo_ready")
        pv_mm = sem("pv_mm")
        o_a = sem("o_a")
        o_v = sem("o_v")
        o_mm = sem("o_mm")
        fin_ready = sem("fin_ready")

        def kview(w):
            return w.rearrange("l (k p) n -> l p k n", p=P)
        ada_v, in_v, co_v, wo_v, wq_v = (kview(w) for w in (ada_w, w_in, w_conv_out, w_out, peer_wq))
        u_v, v_v = (w.rearrange("l (c p) d -> l p c d", p=P) for w in (peer_u, peer_v))
        cw_v = conv_w.rearrange("l k (g p) -> l (k g) p", p=P)
        keys_v = peer_keys.rearrange("l h a n k -> l n (h a) k")
        pw_v = pool_w.rearrange("l g (k p) d -> l p (g k) d", p=P)

        def slot_done(eng, s, l, section, i=0):
            eng.wait_ge(slot_read[s], (l * N_SEC + i) + (section + 2))

        passed = sem("passed")

        def wait_alone(eng, semaphore, value):
            eng.wait_ge(semaphore, value)
            eng.sem_inc(passed, 1)

        block = ctx.enter_context(nc.Block())

        @block.sync
        def _(sp):
            sp.dma_start(val_y[:, :, :].rearrange("p (a k) t -> p a (k t)", a=TT),
                         x[0].rearrange("(a p) d -> p a d", p=P)).then_inc(x_in, 16)

            def load(l, first, i, s, dst, src):
                sp.wait_ge(slot_read[s], (l * N_SEC + i) + (first + 1))
                sp.dma_start(dst, src).then_inc(ring_full[s], 16)

            def stream(l, first, count, source):
                with sp.Fori(0, count) as i:
                    for s in range(SLOTS):
                        load(l, first, i, s, *source(i, s))

            def columns(l, w):
                return lambda i, s: (ring[:, s, :].rearrange("p (k n) -> p k n", k=KD),
                                     w[l, :, :, bass.ds(i * SEC + s * NB, NB)])

            def experts(l, w):
                return lambda i, s: (ring[:, s, :].rearrange("p (c d) -> p c d", c=CPS),
                                     w[l, :, bass.ds(i * CSEC + s * CPS, CPS), :])

            with sp.Fori(0, DEPTH) as l:
                def mixed(first, count, w, sixth):
                    with sp.Fori(0, count) as i:
                        for s in range(SLOTS):
                            src, at = (w, 0) if s < 2 else (ada_v, sixth * SEC)
                            load(l, first, i, s, ring[:, s, :].rearrange("p (k n) -> p k n", k=KD),
                                 src[l, :, :, bass.ds(i * (2 * NB) + (at + s % 2 * NB), NB)])

                def plain(first, w, section):
                    for s in range(SLOTS):
                        load(l, first, 0, s, *columns(l, w)(section, s))

                stream(l, S_ADA01, 2, columns(l, ada_v))
                mixed(S_X, 4, in_v, 2)
                with sp.Fori(0, 3) as i:
                    for s in range(SLOTS):
                        load(l, S_IN2, i, s, *columns(l, in_v)(i + 2, s))
                plain(S_ADA4, ada_v, 4)
                plain(S_CO, co_v, 0)
                plain(S_OUT, wo_v, 0)
                mixed(S_Y, 2, wq_v, 5)
                plain(S_Q1, wq_v, 1)
                stream(l, S_U, USECS, experts(l, u_v))
                stream(l, S_V, USECS, experts(l, v_v))
            sp.wait_ge(fin_ready, 2)
            sp.dma_start(out[0].rearrange("(a p) d -> p a d", p=P), o_sb).then_inc(out_done, 16)
            sp.wait_ge(out_done, 16)

        @block.gpsimd
        def _(pool):
            pool.memset(ident[:, :], 0.0)
            pool.memset(mean_w[:, :], 1.0 / D)
            pool.memset(eps[:, :], EPS)
            pool.memset(ones[:, :], 1.0)
            for t in range(PADP):
                pool.memset(inv_n[:, t:t + 1], 1.0 / (t + 1))
            pool.iota(iota[:, :], pattern=[[1, P]], base=0, channel_multiplier=0,
                      allow_small_or_imprecise_dtypes=True)
            pool.drain()
            pool.affine_select(out=ident[:, :], in_=ident[:, :], compare_op=ALU.not_equal, fill=1.0,
                               base=0, pattern=[[-1, P]], channel_multiplier=1).then_inc(consts_ready, 1)

            with pool.Fori(0, DEPTH) as l:
                wait_alone(pool, x_ready, l * 2 + 1)
                pool.memset(p_pad[:, :, 0:PADP], 0.0)
                wait_alone(pool, z_out, l * (N_IN * KD) + (4 + 3 * KD))
                pool.drain()

                def window(dst, src, g, lo, shift):
                    k = 2 * g
                    end = PADP + T
                    pool.tensor_tensor(dst[:, k:KD, lo:end], src[:, k:KD, lo:end],
                                       src[:, k:KD, lo - shift:end - shift], ALU.add)
                    pool.drain()
                window(win_a, p_pad, 0, 1, 1)
                window(win_b, win_a, 1, 3, 2)
                window(win_a, win_b, 2, 7, 4)
                window(win_b, win_a, 3, 15, 8)
                for g, w in enumerate(WINDOWS):
                    v = (win_a, win_b)[g % 2][:, 2 * g:2 * g + 2, PADP:PADP + T]
                    pool.tensor_scalar(v[:, :, w - 1:T], v[:, :, w - 1:T], 1.0 / w, None, ALU.mult)
                    pool.tensor_tensor(v[:, :, 0:w - 1], v[:, :, 0:w - 1],
                                       inv_n[:, 0:w - 1].unsqueeze(1).broadcast_to([P, 2, w - 1]), ALU.mult)
                pool.drain()
                for g, w in enumerate(WINDOWS):
                    v = (win_a, win_b)[g % 2][:, 2 * g:2 * g + 2, PADP:PADP + T]
                    last = pool.tensor_tensor(v, v,
                                              p_pad[:, 2 * g:2 * g + 2, PADP:PADP + T], ALU.subtract)
                last.then_inc(pooled_ready, 1)

                pool.wait_ge(idx_ready, l + 1)
                wait_alone(pool, s_mm, l * CHUNKS + (CHUNKS + 2))
                with pool.Fori(0, NTG // TB) as i:
                    for n in range(TB):
                        pool.wait_ge(hot2_ready, (l * NTG + i * TB) + (n + 1))
                        pool.tensor_tensor(
                            away[:, n % 2, :, :], iota[:, :].unsqueeze(1).broadcast_to([P, TG, P]),
                            idx_t[:, 2, bass.ds(i * (TB * TG) + n * TG, TG)].unsqueeze(2).broadcast_to([P, TG, P]),
                            ALU.subtract).then_inc(away_ready, 1)

        @block.scalar
        def _(act):
            for l in range(DEPTH):
                at = 0
                for w, n in ((norm1_g, 8), (b_in, 40), (conv_b, 8), (conv_ln_g, 8), (conv_ln_b, 8),
                             (pool_scale, 8), (b_out, 8), (norm2_g, 8)):
                    act.dma_start(rows[at:at + n, 2 * l, :], w[l].rearrange("(r p) -> r p", p=P)).then_inc(rows_in, 16)
                    at += n
                act.dma_start(rows[0:48, 2 * l + 1, :], ada_b[l].rearrange("(r p) -> r p", p=P)).then_inc(rows_in, 16)
                act.dma_start(rows[48:56, 2 * l + 1, :], c[0].rearrange("(r p) -> r p", p=P)).then_inc(rows_in, 16)
                act.dma_start(rows[56:64, 2 * l + 1, :], final_g.rearrange("(r p) -> r p", p=P)).then_inc(rows_in, 16)
            act.sem_inc(z_out, 4)
            act.sem_inc(hot2_ready, 2)
            act.sem_inc(s_act, 2)
            act.sem_inc(ut_hi, 2)
            act.wait_ge(vecs_ready, 1)
            act.activation(c_act[:, :], vecs[:, V_C:V_C + KD], ACT.Silu).then_inc(c_ready, 1)

            def norm_root(l, n, per):
                act.activation(sq[:, :, :], x_t[:, :, :], ACT.Square).then_inc(sq_ready, 1)
                act.wait_ge(mean_mm, l * per + n)
                act.activation(root[:, :], ps[:, 6, 0:T], ACT.Sqrt, bias=eps[:, 0:1]).then_inc(root_ready, 1)

            def round_w(l, n):
                section, s = place(n)
                if n % 2 == 0:
                    act.wait_ge(ring_full[s], l * (N_SEC * 16) + (section + 1) * 16)
                act.wait_ge(part_mm, l * N_W + (n + 1))
                act.activation(by_group(st_hi[:, n % 2, :]), weight_tile(s, n), ACT.Copy).then_inc(w_hi, 1)

            with act.Fori(0, DEPTH) as l:
                act.wait_ge(x_ready, l * 2 + 1)
                for i in range(2):
                    act.dma_start(cw_n[:, i, :], cw_v[l, 124 * i:124 * i + 124, :]).then_inc(small_in, 16)
                for i in range(2):
                    act.dma_start(keys_n[:, KD * i:KD * (i + 1), :],
                                  keys_v[l, :, KD * i:KD * (i + 1), :]).then_inc(small_in, 16)
                act.dma_start(pw[:, :, :], pw_v[l]).then_inc(small_in, 16)
                norm_root(l, 1, 3)
                act.wait_ge(mod_ready, l * 4 + 1)

                def add_shift(at, n):
                    for k in range(KD):
                        act.wait_ge(scaled_ready, l * (3 * KD) + (n + k + 1))
                        act.activation(h_hi[:, k, :], scaled[:, k, :], ACT.Identity, bias=mod[:, at + k:at + k + 1])
                        act.activation(h[:, k, :], scaled[:, k, :], ACT.Identity,
                                       bias=mod[:, at + k:at + k + 1]).then_inc(h_ready, 1)
                add_shift(M_SH1, 0)
                round_w(l, 0)
                for i, (dst, func) in enumerate(((val_y, ACT.Identity), (sq, ACT.Sigmoid), (p_pad, ACT.Identity),
                                                 (gate_a, ACT.Sigmoid), (gate_b, ACT.Sigmoid))):
                    for j in range(KD):
                        n = i * KD + j
                        if n < W_CO:
                            if n + 1 < W_CO:
                                round_w(l, n + 1)
                            act.wait_ge(part_mm, l * N_W + (n + 3))
                        elif j % 2 == 0:
                            slot_done(act, j // 2, l, S_IN2 + i - 2)
                        o = dst[:, j, PADP:PADP + T] if i == 2 else dst[:, j, :]
                        act.activation(o, tile(j), func,
                                       bias=lv[:, V_BIN + n:V_BIN + n + 1]).then_inc(z_out, 1)
                act.wait_ge(cen_ready, l + 1)
                act.activation(sq[:, :, :], conv[:, :, :], ACT.Square).then_inc(sq_ready, 1)
                act.wait_ge(mean_mm, l * 3 + 2)
                act.activation(root[:, :], ps[:, 6, 0:T], ACT.Sqrt, bias=eps[:, 0:1]).then_inc(root_ready, 1)
                for k in range(KD):
                    act.wait_ge(scaled_ready, l * (3 * KD) + (KD + k + 1))
                    act.activation(conv[:, k, :], scaled[:, k, :], ACT.Silu, bias=lv[:, V_LB + k:V_LB + k + 1],
                                   scale=lv[:, V_LG + k:V_LG + k + 1]).then_inc(conv_act, 1)
                for n in range(W_CO, W_OUT + 1):
                    round_w(l, n)
                for j in range(KD):
                    if j + 1 < KD:
                        round_w(l, W_OUT + j + 1)
                    act.wait_ge(part_mm, l * N_W + (W_OUT + j + 3))
                    act.activation(scaled[:, j, :], tile(j), ACT.Identity, bias=g1b[:, j:j + 1],
                                   scale=mod[:, M_G1 + j:M_G1 + j + 1]).then_inc(res_ready, 1)
                act.wait_ge(x_ready, l * 2 + 2)
                norm_root(l, 3, 3)
                add_shift(M_SH2, 2 * KD)
                round_w(l, W_Q)
                for j in range(HP):
                    if j + 1 < HP:
                        round_w(l, W_Q + j + 1)
                    act.wait_ge(part_mm, l * N_W + (W_Q + j + 3))
                    act.activation(q_t[:, j, :], tile(j), ACT.Copy).then_inc(q_out, 1)
                act.wait_ge(score_mm, l * TT + 2)
                act.activation(scores[:, HP * P:2 * HP * P].rearrange("p (b n) -> p b n", n=512),
                               ps[:, 4:8, :], ACT.Copy).then_inc(score_a, 1)

                def round_u(sec, n):
                    sec, n = sec + n // CSEC, n % CSEC
                    cc, b = sec * CSEC + n, n % 2
                    if b == 0:
                        act.wait_ge(ut_mm, (l * (CHUNKS // 2) + sec * (CSEC // 2)) + (n // 2 + 1))
                    else:
                        slot_done(act, n // CPS, l, S_U, sec)
                    act.wait_ge(s_mm, (l * CHUNKS + cc) + 1)
                    act.activation(st_hi[:, b, :].rearrange("p (a n) -> p a n", a=2),
                                   ps[:, 2 * b:2 * b + 2, :], ACT.Copy).then_inc(ut_hi, 1)

                def gelu(cc, b):
                    act.wait_ge(s_mm, (l * CHUNKS + cc) + 3)
                    act.activation(gs[:, bass.ds(cc * T, T)], ps[:, 4 + b, 0:T], ACT.Gelu).then_inc(s_act, 1)

                def u_section(i, last=False):
                    for n in range(CSEC):
                        if not (last and n == CSEC - 1):
                            round_u(i, n + 1)
                        gelu(i * CSEC + n, n % 2)

                round_u(0, 0)
                with act.Fori(0, 10) as i:
                    u_section(i)
                act.wait_ge(logits_ready, l + 1)
                act.activation(expo, shifted, ACT.Exp).then_inc(expo_ready, 1)
                with act.Fori(10, USECS - 1) as i:
                    u_section(i)
                u_section(USECS - 1, last=True)

                with act.Fori(0, NTG // TB) as i:
                    for n in range(TB):
                        b = n % 2
                        act.wait_ge(away_ready, (l * NTG + i * TB) + (n + 1))
                        act.activation(away[:, b, :, :], away[:, b, :, :], ACT.Abs)
                        act.drain()
                        act.wait_ge(w_mm, (l * NTG + i * TB) + (n + 1))
                        act.activation(hot2[:, b, :, :], away[:, b, :, :], ACT.Relu, bias=1.0,
                                       scale=-1.0).then_inc(hot2_ready, 1)
                act.wait_ge(w_used, l * NTG + (NTG + 2))
                with act.Fori(0, USECS) as i:
                    for n in range(CSEC):
                        b = n % 2
                        if n % CPS == 0:
                            act.wait_ge(ring_full[n // CPS], (l * N_SEC + i) * 16 + (S_V + 1) * 16)
                        act.wait_ge(pv_mm, (l * CHUNKS + i * CSEC) + (n + 1))
                        act.activation(st_hi[:, b, :], ring[:, n // CPS, b * D:(b + 1) * D], ACT.Copy)
                        act.activation(p_hi[:, b, :], gs[:, bass.ds(i * (CSEC * T) + n * T, T)],
                                       ACT.Copy).then_inc(v_hi_ready, 1)
                act.wait_ge(pv_mm, l * CHUNKS + (CHUNKS + 2))
                act.activation(o_sb[:, 0, :].rearrange("p (a n) -> p a n", a=2), ps[:, 0:2, :], ACT.Copy).then_inc(o_a, 1)

            act.wait_ge(x_ready, 2 * DEPTH + 1)
            norm_root(0, 3 * DEPTH + 1, 0)
            act.wait_ge(o_mm, DEPTH + 1)
            act.activation(o_sb[:, 0, :].rearrange("p (a n) -> p a n", a=2), ps[:, 0:2, :], ACT.Copy).then_inc(fin_ready, 1)

        @block.vector
        def _(dve):
            dve.sem_inc(ut_lo, 2)
            dve.sem_inc(w_used, 2)
            dve.wait_ge(start_mm, 1)
            for l in range(DEPTH):
                dve.tensor_copy(vecs[:, l * NVEC:l * NVEC + ROWS_A], ps[:, 2 * l, 0:ROWS_A])
                last = dve.tensor_copy(vecs[:, l * NVEC + ROWS_A:(l + 1) * NVEC], ps[:, 2 * l + 1, 0:ROWS_B])
            last.then_inc(vecs_ready, 1)
            dve.wait_ge(start_mm, 2)
            dve.tensor_copy(x_t[:, :, :].rearrange("p (b c) t -> p b (c t)", c=2), ps[:, 4:8, :]).then_inc(x_ready, 1)

            def norm_scale(l, n, gain):
                dve.wait_ge(root_ready, n)
                dve.reciprocal(rs[:, :], root[:, :])
                dve.drain()
                for k in range(KD):
                    dve.scalar_tensor_tensor(scaled[:, k, :], x_t[:, k, :], gain(k), rs[:, :], ALU.mult,
                                             ALU.mult).then_inc(scaled_ready, 1)

            with dve.Fori(0, DEPTH) as l:
                dve.wait_ge(x_ready, l * 2 + 1)
                dve.tensor_copy(lv[:, :], vecs[:, bass.ds(l * NVEC, NVEC)])
                dve.memset(u_pad[:, :, 0:PADC], 0.0)
                dve.wait_ge(setup_mm, l + 1)
                dve.tensor_copy(keys_t[:, :, :].rearrange("p (b c) n -> p b (c n)", c=4), ps[:, 0:4, :])
                dve.tensor_copy(cw[:, :], ps[:, 4, 0:2 * 124]).then_inc(setup_ready, 1)
                dve.drain()
                def ada_products(section, slots, dst, at, p):
                    s0, s1 = slots
                    o = dst[:, at:at + 2 * NB].rearrange("p (s n) -> p s n", s=2)
                    for s in slots:
                        dve.wait_ge(ring_full[s], l * (N_SEC * 16) + (section + 1) * 16)
                    for k in range(KD):
                        w = ring[:, s0:s1 + 1, k * NB:(k + 1) * NB]
                        if k == 0:
                            last = dve.tensor_scalar(o, w, c_act[:, 0:1], None, ALU.mult)
                        else:
                            dve.drain()
                            last = dve.scalar_tensor_tensor(o, w, c_act[:, k:k + 1], o, ALU.mult, ALU.add)
                    last.then_inc(slot_read[s0], 1)
                    dve.drain().then_inc(slot_read[s1], 1)
                    if p:
                        dve.drain().then_inc(ada_part, 1)

                def rest_w(n):
                    section, s = place(n)
                    dve.wait_ge(w_hi, l * N_W + (n + 1))
                    dve.tensor_tensor(by_group(st_lo[:, n % 2, :]), weight_tile(s, n),
                                      by_group(st_hi[:, n % 2, :]).bitcast(F32),
                                      ALU.subtract).then_inc(slot_read[s] if n % 2 else w_lo, 1)

                def rest_h(n):
                    for k in range(KD):
                        dve.wait_ge(h_ready, l * (2 * KD) + (n + k + 1))
                        last = dve.tensor_tensor(h_lo[:, k, :], h[:, k, :], h_hi[:, k, :].bitcast(F32), ALU.subtract)
                    last.then_inc(x_lo_ready, 1)

                def parts(src):
                    dve.tensor_copy(h_hi[:, :, :], src).then_inc(x_hi_ready, 1)
                    dve.drain()
                    dve.tensor_tensor(h_lo[:, :, :], src, h_hi[:, :, :].bitcast(F32), ALU.subtract).then_inc(x_lo_ready, 1)

                def take_mod(a0, a1):
                    dve.wait_ge(ada_mm, l * N_ADA + a1)
                    dve.tensor_tensor(mod[:, a0 * KD:a1 * KD], ps[:, 7, a0 * KD:a1 * KD],
                                      lv[:, V_ADAB + a0 * KD:V_ADAB + a1 * KD], ALU.add)
                    dve.drain()

                for a in range(2):
                    for q in range(2):
                        ada_products(S_ADA01 + a, (2 * q, 2 * q + 1), ada_acc[:, a, :], q * 2 * NB, q)
                take_mod(0, 2)
                dve.scalar_tensor_tensor(amp[:, 0, :], mod[:, M_SC1:M_SC1 + KD], 1.0, lv[:, V_N1:V_N1 + KD], ALU.add,
                                         ALU.mult).then_inc(mod_ready, 1)
                dve.drain()
                norm_scale(l, l * 3 + 1, lambda k: amp[:, 0, k:k + 1])
                rest_h(0)
                for x in range(4):
                    for n in range(4):
                        rest_w(4 * x + n)
                    ada_products(S_X + x, (2, 3), ada_acc[:, x // 2, :], x % 2 * 2 * NB, x % 2)
                for j in range(KD):
                    dve.wait_ge(z_out, l * (N_IN * KD) + (4 + KD + j + 1))
                    dve.tensor_tensor(u_pad[:, j, PADC:PADC + T], val_y[:, j, :], sq[:, j, :], ALU.mult)
                dve.drain()
                for k in range(KD):
                    dve.tensor_scalar(conv[:, k, :], u_pad[:, k, 0:T], cw[:, k:k + 1],
                                      lv[:, V_CB + k:V_CB + k + 1], ALU.mult, ALU.add)
                with dve.Fori(1, TAPS) as tap:
                    dve.drain()
                    for k in range(KD):
                        dve.scalar_tensor_tensor(conv[:, k, :], u_pad[:, k, bass.ds(tap, T)],
                                                 cw[:, bass.ds(tap * KD + k, 1)], conv[:, k, :], ALU.mult, ALU.add)
                dve.drain().then_inc(conv_ready, 1)
                take_mod(2, 4)
                dve.tensor_tensor(g1b[:, :], mod[:, M_G1:M_G1 + KD], lv[:, V_BO:V_BO + KD], ALU.mult).then_inc(mod_ready, 1)
                dve.wait_ge(cen_mm, l + 1)
                dve.tensor_tensor(conv[:, :, :], conv[:, :, :], ps[:, 5, 0:T].unsqueeze(1).broadcast_to([P, KD, T]),
                                  ALU.subtract).then_inc(cen_ready, 1)
                for j in range(KD):
                    if j % 2 == 0:
                        dve.wait_ge(pool_mm, l * (KD // 2) + (j // 2 + 1))
                    dve.scalar_tensor_tensor(pool_out[:, j, :], pair(j),
                                             lv[:, V_PS + j:V_PS + j + 1], gate_b[:, j, :], ALU.mult,
                                             ALU.mult).then_inc(pool_ready, 1)
                for q in range(2):
                    ada_products(S_ADA4, (2 * q, 2 * q + 1), ada_acc2[:, 0, :], q * 2 * NB, q)
                dve.wait_ge(root_ready, l * 3 + 2)
                dve.reciprocal(rs[:, :], root[:, :])
                dve.drain()
                for k in range(KD):
                    dve.tensor_tensor(scaled[:, k, :], conv[:, k, :], rs[:, :], ALU.mult).then_inc(scaled_ready, 1)
                dve.wait_ge(conv_act, l * KD + KD)
                parts(conv[:, :, :])
                rest_w(W_CO)
                for j in range(KD):
                    if j + 1 < KD:
                        rest_w(W_CO + j + 1)
                    dve.wait_ge(part_mm, l * N_W + (W_CO + j + 3))
                    dve.tensor_tensor(val_y[:, j, :], tile(j), gate_a[:, j, :], ALU.mult).then_inc(y_out, 1)
                dve.drain()
                dve.tensor_tensor(val_y[:, :, :], val_y[:, :, :], pool_out[:, :, :], ALU.add)
                dve.drain()
                parts(val_y[:, :, :])
                rest_w(W_OUT)
                take_mod(4, 5)
                dve.scalar_tensor_tensor(amp[:, 1, :], mod[:, M_SC2:M_SC2 + KD], 1.0, lv[:, V_N2:V_N2 + KD],
                                         ALU.add, ALU.mult).then_inc(mod_ready, 1)
                for j in range(KD):
                    if j + 1 < KD:
                        rest_w(W_OUT + j + 1)
                    dve.wait_ge(res_ready, l * KD + (j + 1))
                    last = dve.tensor_tensor(x_t[:, j, :], x_t[:, j, :], scaled[:, j, :], ALU.add)
                last.then_inc(x_ready, 1)
                norm_scale(l, l * 3 + 3, lambda k: amp[:, 1, k:k + 1])
                rest_h(KD)
                for x in range(2):
                    for n in range(4):
                        rest_w(W_Q + 4 * x + n)
                    ada_products(S_Y + x, (2, 3), ada_acc2[:, 1, :], x * 2 * NB, x)
                for n in range(KD):
                    rest_w(W_Q + KD + n)
                take_mod(5, 6)
                dve.drain().then_inc(mod_ready, 1)
                dve.wait_ge(score_mm, l * TT + 1)
                dve.tensor_copy(scores[:, 0:HP * P].rearrange("p (b n) -> p b n", n=512), ps[:, 0:4, :]).then_inc(score_v, 1)
                wait_alone(dve, score_a, l + 1)

                def rest_u(cc, b):
                    dve.wait_ge(ut_hi, (l * CHUNKS + cc) + 3)
                    dve.tensor_tensor(st_lo[:, b, :].rearrange("p (a n) -> p a n", a=2), ps[:, 2 * b:2 * b + 2, :],
                                      st_hi[:, b, :].bitcast(F32).rearrange("p (a n) -> p a n", a=2),
                                      ALU.subtract).then_inc(ut_lo, 1)

                def top16(values, spare, n_idx):
                    dve.max(best_v[:, 0:8], values)
                    dve.drain()
                    dve.match_replace(out=spare, in_to_replace=best_v[:, 0:8], in_values=values, imm_value=NEG)
                    dve.max_index(n_idx[:, 0:8], best_v[:, 0:8], values)
                    dve.drain()
                    dve.max(best_v[:, 8:16], spare)
                    dve.drain()
                    dve.max_index(n_idx[:, 8:16], best_v[:, 8:16], spare)
                    dve.drain()

                with dve.Fori(0, 4) as i:
                    for n in range(CSEC):
                        rest_u(i * CSEC + n, n % 2)
                        dve.tensor_copy(work, scores[:, bass.ds(i * (CSEC * P) + n * P, P)])
                        dve.drain()
                        top16(work, work2, best_i)
                        dve.tensor_copy(top_v[:, bass.ds(i * (CSEC * TOPK) + n * TOPK, TOPK)], best_v)
                        dve.tensor_copy(top_i[:, bass.ds(i * (CSEC * TOPK) + n * TOPK, TOPK)], best_i)
                dve.drain()
                with dve.Fori(0, 8) as i:
                    for n in range(6):
                        rest_u(i * 6 + (4 * CSEC + n), n % 2)
                        at = i * (4 * TOPK) + (n // 3) * 2 * TOPK
                        th = i * (2 * TOPK) + (n // 3) * TOPK
                        if n % 3 == 0:
                            dve.tensor_tensor(
                                cand.rearrange("p (i j) -> p i j", i=TOPK),
                                top_v[:, bass.ds(at, TOPK)].unsqueeze(2).broadcast_to([P, TOPK, TOPK]),
                                top_v[:, bass.ds(at + TOPK, TOPK)].unsqueeze(1).broadcast_to([P, TOPK, TOPK]), ALU.add)
                            dve.drain()
                            top16(cand, cand2, best_i)
                            dve.tensor_copy(logits[:, bass.ds(th, TOPK)], best_v)
                        else:
                            half = n % 3 - 1
                            a, op = ((4, ALU.logical_shift_right), (TOPK - 1, ALU.bitwise_and))[half]
                            dve.tensor_scalar(pos, best_i, a, None, op)
                            dve.drain()
                            dve.tensor_copy(pos_f, pos)
                            dve.drain()
                            hot = pick_hot.rearrange("p (k j) -> p k j", k=TOPK)
                            hot_b = pick_hot2.rearrange("p (k j) -> p k j", k=TOPK)
                            dve.tensor_tensor(hot, pos_f.unsqueeze(2).broadcast_to([P, TOPK, TOPK]),
                                              iota[:, 0:TOPK].unsqueeze(1).broadcast_to([P, TOPK, TOPK]), ALU.is_equal)
                            dve.drain()
                            dve.tensor_tensor(hot_b, hot, top_i[:, bass.ds(at + half * TOPK, TOPK)].unsqueeze(1)
                                              .broadcast_to([P, TOPK, TOPK]), ALU.mult)
                            dve.drain()
                            dve.tensor_reduce(picks[:, bass.ds(th + half * (2 * T), TOPK)], hot_b, axis=AX.X, op=ALU.add)
                dve.drain()
                by_head = dict(k=TOPK)
                dve.tensor_tensor(shifted.rearrange("p (g k) -> p g k", **by_head),
                                  logits.rearrange("p (g k) -> p g k", **by_head),
                                  logits.rearrange("p (g k) -> p g k", **by_head)[:, :, 0:1].broadcast_to(
                                      [P, TT * HEADS, TOPK]), ALU.subtract).then_inc(logits_ready, 1)
                with dve.Fori(0, CSEC // 2) as i:
                    for n in range(2):
                        rest_u(i * 2 + (10 * CSEC + n), n)
                dve.wait_ge(expo_ready, l + 1)
                dve.tensor_reduce(total, expo.rearrange("p (g k) -> p g k", **by_head), axis=AX.X, op=ALU.add)
                dve.drain()
                dve.reciprocal(total_r, total)
                dve.drain()
                dve.tensor_tensor(picks[:, T:2 * T].rearrange("p (g k) -> p g k", **by_head),
                                  expo.rearrange("p (g k) -> p g k", **by_head),
                                  total_r.unsqueeze(2).broadcast_to([P, TT * HEADS, TOPK]), ALU.mult).then_inc(picks_ready, 1)
                with dve.Fori(0, CSEC // 2) as i:
                    for n in range(2):
                        rest_u(i * 2 + (11 * CSEC + n), n)
                dve.wait_ge(picks_mm, l + 1)
                dve.tensor_copy(idx_t[:, 0:2, :], ps[:, 6, :].rearrange("p (a t) -> p a t", a=2))
                dve.tensor_copy(idx_t[:, 2, :], ps[:, 7, 0:T]).then_inc(idx_ready, 1)
                with dve.Fori(12, USECS) as i:
                    for n in range(CSEC):
                        rest_u(i * CSEC + n, n % 2)

                def own_rows(first, n):
                    dve.drain()
                    dve.tensor_copy(own[:, :, 0:n], idx_t[:, 0:2, bass.ds(first, n)])
                    dve.drain()

                def hot_rows(n):
                    for k in range(TG):
                        t = n * TG + k
                        last = dve.tensor_scalar(hot1[:, n % 2, k, :], iota[:, :], own[:, 0, t:t + 1],
                                                 own[:, 1, t:t + 1], ALU.is_equal, ALU.mult)
                    last.then_inc(hot1_ready, 1)

                def weigh(g, b):
                    dve.wait_ge(w_mm, (l * NTG + g) + 3)
                    acts = gs[:, :].rearrange("p (c t) -> p t c", t=T)[:, bass.ds(g * TG, TG), :]
                    dve.tensor_tensor(acts, acts, ps[:, b, :].rearrange("p (t c) -> p t c", t=TG),
                                      ALU.mult).then_inc(w_used, 1)

                own_rows(0, 2 * TG)
                dve.wait_ge(s_act, l * CHUNKS + (CHUNKS + 2))
                hot_rows(0)
                hot_rows(1)
                with dve.Fori(0, NTG // TB - 1) as i:
                    own_rows(i * (TB * TG) + 2 * TG, TB * TG)
                    for n in range(TB):
                        weigh(i * TB + n, n % 2)
                        hot_rows(n)
                own_rows(T - 2 * TG, 2 * TG)
                for n in range(TB):
                    weigh(NTG - TB + n, n % 2)
                    if n < 2:
                        hot_rows(n)
                dve.drain()

                with dve.Fori(0, USECS) as i:
                    for n in range(CSEC):
                        b = n % 2
                        dve.wait_ge(v_hi_ready, (l * CHUNKS + i * CSEC) + (n + 1))
                        v = dve.tensor_tensor(st_lo[:, b, :], ring[:, n // CPS, b * D:(b + 1) * D],
                                              st_hi[:, b, :].bitcast(F32), ALU.subtract)
                        if b == CPS - 1:
                            v.then_inc(slot_read[n // CPS], 1)
                        dve.tensor_tensor(p_lo[:, b, :], gs[:, bass.ds(i * (CSEC * T) + n * T, T)],
                                          p_hi[:, b, :].bitcast(F32), ALU.subtract).then_inc(v_lo_ready, 1)
                dve.wait_ge(pv_mm, l * CHUNKS + (CHUNKS + 2))
                dve.tensor_copy(o_sb[:, 1, :].rearrange("p (a n) -> p a n", a=2), ps[:, 2:4, :]).then_inc(o_v, 1)
                dve.wait_ge(o_mm, l + 1)
                for k in range(KD):
                    last = dve.scalar_tensor_tensor(x_t[:, k, :], ps[:, 4 + k // 2, (k % 2) * T:(k % 2 + 1) * T],
                                                    mod[:, M_G2 + k:M_G2 + k + 1], x_t[:, k, :], ALU.mult, ALU.add)
                last.then_inc(x_ready, 1)

            norm_scale(0, 3 * DEPTH + 1, lambda k: vecs[:, V_FG + k:V_FG + k + 1])
            dve.wait_ge(o_mm, DEPTH + 1)
            dve.tensor_copy(o_sb[:, 1, :].rearrange("p (a n) -> p a n", a=2), ps[:, 2:4, :]).then_inc(fin_ready, 1)

        @block.tensor
        def _(pe):
            for s in range(SLOTS):
                pe.sem_inc(slot_read[s], 1)
            pe.sem_inc(part_mm, 2)
            pe.sem_inc(s_mm, 2)
            pe.sem_inc(w_mm, 2)
            pe.sem_inc(pv_mm, 2)
            pe.wait_ge(consts_ready, 1)
            pe.wait_ge(rows_in, 16 * 11 * DEPTH)
            for l in range(DEPTH):
                pe.transpose(ps[:, 2 * l, 0:ROWS_A], rows[0:ROWS_A, 2 * l, :], ident[0:ROWS_A, 0:ROWS_A])
                last = pe.transpose(ps[:, 2 * l + 1, 0:ROWS_B], rows[0:ROWS_B, 2 * l + 1, :], ident[0:ROWS_B, 0:ROWS_B])
            last.then_inc(start_mm, 1)
            pe.wait_ge(x_in, 16)
            xin = val_y[:, :, :].rearrange("p (a k) t -> p a (k t)", a=TT)

            def to_channels(src):
                for k in range(KD):
                    for a in range(TT):
                        last = pe.transpose(ps[:, 4 + k // 2, (k % 2) * T + a * P:(k % 2) * T + (a + 1) * P],
                                            src[:, a, k * P:(k + 1) * P], ident[:, :])
                return last
            to_channels(xin).then_inc(start_mm, 1)
            pe.wait_ge(c_ready, 1)

            def mean_of(src, bank):
                for k in range(KD):
                    last = pe.matmul(ps[:, bank, 0:T], mean_w[:, :], src[:, k, :], start=(k == 0), stop=(k == KD - 1))
                return last

            def section(l, first, i, src, before):
                for j in range(KD):
                    s, half = j // 2, j % 2
                    if half == 0:
                        pe.wait_ge(ring_full[s], (l * N_SEC + i) * 16 + (first + 1) * 16)
                    before(j)
                    for k in range(KD):
                        last = pe.matmul(tile(j), ring[:, s, k * NB + half * P:k * NB + (half + 1) * P],
                                         src[:, k, :], start=(k == 0), stop=(k == KD - 1))
                    if half:
                        last.then_inc(slot_read[s], 1)

            def ada_sum(l, a):
                pe.wait_ge(ada_part, l * N_ADA + (a + 1))
                acc = ada_acc2[:, a - 4, :] if a >= 4 else ada_acc[:, a % 2, :]
                for j in range(KD):
                    last = pe.matmul(ps[:, 7, a * KD + j:a * KD + j + 1], acc[:, j * P:(j + 1) * P], ones[:, 0:1],
                                     start=True, stop=True)
                last.then_inc(ada_mm, 1)

            def split_tile(l, n, before=None):
                b, (section, s) = n % 2, place(n)
                pe.wait_ge(w_hi, l * N_W + (n + 1))
                if before:
                    before()
                for k in range(KD):
                    pe.matmul(tile(n), st_hi[:, b, k * P:(k + 1) * P], h_hi[:, k, :], start=(k == 0), stop=False)
                if b:
                    slot_done(pe, s, l, section)
                else:
                    pe.wait_ge(w_lo, l * (N_W // 2) + (n // 2 + 1))
                for k in range(KD):
                    pe.matmul(tile(n), st_lo[:, b, k * P:(k + 1) * P], h_hi[:, k, :], start=False, stop=False)
                pe.wait_ge(x_lo_ready, l * 4 + (1 if n < W_CO else 2 if n < W_OUT else 3 if n < W_Q else 4))
                for k in range(KD):
                    last = pe.matmul(tile(n), st_hi[:, b, k * P:(k + 1) * P], h_lo[:, k, :], start=False,
                                     stop=(k == KD - 1))
                last.then_inc(part_mm, 1)

            with pe.Fori(0, DEPTH) as l:
                pe.wait_ge(x_ready, l * 2 + 1)
                pe.wait_ge(small_in, l * (5 * 16) + 5 * 16)
                for j in range(HP):
                    pe.transpose(ps[:, j // 4, (j % 4) * P:(j % 4 + 1) * P], keys_n[:, j, :], ident[:, :])
                for i in range(2):
                    last = pe.transpose(ps[:, 4, i * 124:(i + 1) * 124], cw_n[:, i, :], ident[0:124, 0:124])
                last.then_inc(setup_mm, 1)
                pe.wait_ge(sq_ready, l * 3 + 1)
                mean_of(sq, 6).then_inc(mean_mm, 1)
                ada_sum(l, 0)
                ada_sum(l, 1)
                pe.wait_ge(setup_ready, l + 1)
                pe.wait_ge(h_ready, l * (2 * KD) + KD)
                for n in range(W_CO):
                    split_tile(l, n, lambda: pe.wait_ge(z_out, l * (N_IN * KD) + (n + 1)))
                ada_sum(l, 2)
                ada_sum(l, 3)
                with pe.Fori(0, N_IN - 2) as i:
                    section(l, S_IN2, i, h, lambda j: pe.wait_ge(z_out, (l * (N_IN * KD) + i * KD) + (2 * KD + j + 1)))
                pe.wait_ge(pooled_ready, l + 1)
                pe.wait_ge(z_out, l * (N_IN * KD) + (N_IN * KD + 4))
                for j in range(KD):
                    g, half = j // 2, j % 2
                    for k in range(2):
                        last = pe.matmul(pair(j),
                                         pw[:, 2 * g + k, half * P:(half + 1) * P],
                                         (win_a, win_b)[g % 2][:, 2 * g + k, PADP:PADP + T],
                                         start=(k == 0), stop=(k == 1))
                    if half:
                        last.then_inc(pool_mm, 1)
                pe.wait_ge(conv_ready, l + 1)
                mean_of(conv, 5).then_inc(cen_mm, 1)
                pe.wait_ge(sq_ready, l * 3 + 2)
                mean_of(sq, 6).then_inc(mean_mm, 1)
                pe.wait_ge(mod_ready, l * 4 + 2)
                ada_sum(l, 4)
                pe.wait_ge(pool_ready, l * KD + KD)
                pe.wait_ge(x_hi_ready, l * 2 + 1)

                def bank_of(sem_, n):
                    return (lambda: pe.wait_ge(sem_, l * KD + (n % KD - 3))) if n % KD >= 4 else None
                for n in range(W_CO, W_OUT):
                    split_tile(l, n, bank_of(y_out, n))
                pe.wait_ge(x_hi_ready, l * 2 + 2)
                for n in range(W_OUT, W_Q):
                    split_tile(l, n, bank_of(res_ready, n))
                pe.wait_ge(sq_ready, l * 3 + 3)
                mean_of(sq, 6).then_inc(mean_mm, 1)
                pe.wait_ge(h_ready, l * (2 * KD) + 2 * KD)
                for n in range(HP):
                    split_tile(l, W_Q + n, (lambda: pe.wait_ge(q_out, l * HP + (n - 3))) if n >= 4 else None)
                pe.wait_ge(mod_ready, l * 4 + 3)
                ada_sum(l, 5)
                pe.wait_ge(q_out, l * HP + HP)
                pe.wait_ge(mod_ready, l * 4 + 4)
                for a in range(TT):
                    for j in range(HP):
                        last = pe.matmul(ps[:, 4 * a + j // 4, (j % 4) * P:(j % 4 + 1) * P],
                                         q_t[:, j, a * P:(a + 1) * P], keys_t[:, j, :], start=True, stop=True)
                    last.then_inc(score_mm, 1)
                pe.wait_ge(score_v, l + 1)
                pe.wait_ge(score_a, l + 1)

                def turn_u(sec, n):
                    sec, n = sec + n // CSEC, n % CSEC
                    cc, b, s = sec * CSEC + n, n % 2, n // CPS
                    if n % CPS == 0:
                        pe.wait_ge(ring_full[s], (l * N_SEC + sec) * 16 + (S_U + 1) * 16)
                    pe.wait_ge(ut_hi, (l * CHUNKS + cc) + 1)
                    pe.wait_ge(ut_lo, (l * CHUNKS + cc) + 1)
                    for k in range(KD):
                        last = pe.transpose(ps[:, 2 * b + k // 4, (k % 4) * P:(k % 4 + 1) * P],
                                            ring[:, s, b * D + k * P:b * D + (k + 1) * P], ident[:, :])
                    last.then_inc(slot_read[s] if b == CPS - 1 else ut_mm, 1)

                def use_u(sec, n):
                    cc, b = sec * CSEC + n, n % 2
                    o = ps[:, 4 + b, 0:T]
                    pe.wait_ge(s_act, (l * CHUNKS + cc) + 1)
                    pe.wait_ge(ut_hi, (l * CHUNKS + cc) + 3)
                    for k in range(KD):
                        pe.matmul(o, st_hi[:, b, k * P:(k + 1) * P], h_hi[:, k, :], start=(k == 0), stop=False)
                        pe.matmul(o, st_hi[:, b, k * P:(k + 1) * P], h_lo[:, k, :], start=False, stop=False)
                    pe.wait_ge(ut_lo, (l * CHUNKS + cc) + 3)
                    for k in range(KD):
                        last = pe.matmul(o, st_lo[:, b, k * P:(k + 1) * P], h_hi[:, k, :], start=False, stop=(k == KD - 1))
                    last.then_inc(s_mm, 1)

                def u_section(i, last=False):
                    for n in range(CSEC):
                        if not (last and n == CSEC - 1):
                            turn_u(i, n + 1)
                        use_u(i, n)
                turn_u(0, 0)
                with pe.Fori(0, 12) as i:
                    u_section(i)
                pe.wait_ge(picks_ready, l + 1)
                for a in range(3):
                    for t in range(TT):
                        last = pe.transpose(ps[:, 6 + a // 2, (a % 2) * T + t * P:(a % 2) * T + (t + 1) * P],
                                            picks[:, a * T + t * P:a * T + (t + 1) * P], ident[:, :])
                last.then_inc(picks_mm, 1)
                with pe.Fori(12, USECS - 1) as i:
                    u_section(i)
                u_section(USECS - 1, last=True)

                with pe.Fori(0, NTG // TB) as i:
                    for n in range(TB):
                        b = n % 2
                        pe.wait_ge(w_used, (l * NTG + i * TB) + (n + 1))
                        pe.wait_ge(hot1_ready, (l * NTG + i * TB) + (n + 1))
                        pe.wait_ge(hot2_ready, (l * NTG + i * TB) + (n + 3))
                        for k in range(TG):
                            last = pe.matmul(ps[:, b, k * P:(k + 1) * P], hot2[:, b, k, :], hot1[:, b, k, :],
                                             start=True, stop=True)
                        last.then_inc(w_mm, 1)

                pe.wait_ge(w_used, l * NTG + (NTG + 2))

                def v_section(i, first=False, final=False):
                    for n in range(CSEC):
                        b = n % 2
                        start, stop = first and n == 0, final and n == CSEC - 1
                        pe.wait_ge(v_hi_ready, (l * CHUNKS + i * CSEC) + (n + 1))
                        for a in range(TT):
                            for hf in range(2):
                                pe.matmul(ps[:, 2 * a + hf, :], p_hi[:, b, a * P:(a + 1) * P],
                                          st_hi[:, b, hf * 512:(hf + 1) * 512], start=start, stop=False)
                        pe.wait_ge(v_lo_ready, (l * CHUNKS + i * CSEC) + (n + 1))
                        for a in range(TT):
                            for hf in range(2):
                                pe.matmul(ps[:, 2 * a + hf, :], p_hi[:, b, a * P:(a + 1) * P],
                                          st_lo[:, b, hf * 512:(hf + 1) * 512], start=False, stop=False)
                            for hf in range(2):
                                last = pe.matmul(ps[:, 2 * a + hf, :], p_lo[:, b, a * P:(a + 1) * P],
                                                 st_hi[:, b, hf * 512:(hf + 1) * 512], start=False, stop=stop)
                        last.then_inc(pv_mm, 1)
                v_section(0, first=True)
                with pe.Fori(1, USECS - 1) as i:
                    v_section(i)
                v_section(USECS - 1, final=True)
                pe.wait_ge(o_a, l + 1)
                pe.wait_ge(o_v, l + 1)
                to_channels(o_sb).then_inc(o_mm, 1)

            pe.wait_ge(sq_ready, 3 * DEPTH + 1)
            mean_of(sq, 6).then_inc(mean_mm, 1)
            for k in range(KD):
                pe.wait_ge(scaled_ready, DEPTH * 3 * KD + k + 1)
                for a in range(TT):
                    last = pe.transpose(ps[:, 2 * a + k // 4, (k % 4) * P:(k % 4 + 1) * P],
                                        scaled[:, k, a * P:(a + 1) * P], ident[:, :])
            last.then_inc(o_mm, 1)


_INS = ["x", "c", "ada_w", "ada_b", "norm1_g", "w_in", "b_in", "conv_w", "conv_b", "conv_ln_g", "conv_ln_b",
        "w_conv_out", "pool_w", "pool_scale", "w_out", "b_out", "norm2_g", "peer_wq", "peer_keys", "peer_u",
        "peer_v", "final_g"]


def kernel(**inputs):
    import concourse.bacc as bacc
    from concourse.bass_utils import run_bass_kernel_spmd

    nc = bacc.Bacc("TRN2", target_bir_lowering=False, num_devices=1)
    arrays, args = {}, []
    for name in _INS:
        a = np.ascontiguousarray(inputs[name])
        arrays[f"in_{name}"] = a
        args.append(nc.dram_tensor(f"in_{name}", a.shape, mybir.dt.from_np(a.dtype), kind="ExternalInput").ap())
    args.append(nc.dram_tensor("out_x", (1, T, D), F32, kind="ExternalOutput").ap())
    build(nc, *args)
    r = run_bass_kernel_spmd(nc, [arrays], core_ids=[0])
    return r.results[0]["out_x"]
```

```python
import numpy as np
import concourse.bass as bass
from concourse import mybir
from concourse.alu_op_type import AluOpType as ALU
from contextlib import ExitStack

F32 = mybir.dt.float32
F32R = mybir.dt.float32r
U32 = mybir.dt.uint32
ACT = mybir.ActivationFunctionType
AX = mybir.AxisListType

P = 128
D = 1024
T = 256
DEPTH = 2
KD = D // P
KP = 3
KV = KD - KP
TT = T // P
TAPS = 31
PADC = TAPS - 1
WINDOWS = (2, 4, 8, 16)
PADP = 16
HEADS = 8
HP = 2 * HEADS
NKEYS = 128
TOPK = 16
CHUNKS = NKEYS
EPS = 1e-6
NEG = -3.0e38

SLOTS = 4
SLOT = 2048
SEC = 1024
NB = SEC // SLOTS
CPS = 2
CSEC = SLOTS * CPS
USECS = CHUNKS // CSEC

N_ADA, N_IN = 6, 5
S_ADA01 = 0
S_X = 2
S_CO = 10
S_OUT = 11
S_Y = 12
S_Q1 = 14
S_U = 15
S_V = S_U + USECS
N_SEC = S_V + USECS

W_IN, W_CO, W_OUT, W_Q, N_W = 0, 16, 24, 32, 48


X_SECTIONS = ((("in", 0), ("in", 1), ("ada", 8), ("ada", 9)),
              (("in", 2), ("in", 3), ("in", 4), ("in", 5)),
              (("ada", 10), ("ada", 11), ("in", 6), ("in", 7)),
              (("in", 8), ("in", 9), ("ada", 12), ("ada", 13)),
              (("in", 10), ("in", 11), ("in", 12), ("in", 13)),
              (("ada", 14), ("ada", 15), ("in", 14), ("in", 15)),
              (("in", 16), ("in", 17), ("ada", 16), ("ada", 17)),
              (("in", 18), ("in", 19), ("ada", 18), ("ada", 19)))
X_PLACE = {block: (S_X + i, s) for i, slots in enumerate(X_SECTIONS) for s, block in enumerate(slots)}


def place(n):
    if n < W_CO:
        return X_PLACE["in", n // 2]
    if n < W_Q:
        return (S_CO if n < W_OUT else S_OUT), n % 8 // 2
    if n < W_Q + KD:
        return S_Y + (n - W_Q) // 4, n % 4 // 2
    return S_Q1, n % 8 // 2


V_N1, V_BIN, V_CB, V_LG, V_LB, V_PS, V_BO, V_N2 = 0, 8, 48, 56, 64, 72, 80, 88
ROWS_A = 96
V_ADAB, V_C, V_FG = ROWS_A, ROWS_A + 48, ROWS_A + 56
ROWS_B = 64
NVEC = ROWS_A + ROWS_B
M_SH1, M_SC1, M_G1, M_SH2, M_SC2, M_G2 = (KD * i for i in range(6))

TG = 4
NTG = T // TG
TB = 4


def build(nc, x, c, ada_w, ada_b, norm1_g, w_in, b_in, conv_w, conv_b, conv_ln_g, conv_ln_b, w_conv_out,
          pool_w, pool_scale, w_out, b_out, norm2_g, peer_wq, peer_keys, peer_u, peer_v, final_g, out):
    ctx = ExitStack()
    with ctx:
        def sb(name, shape, dt=F32, stack=ctx):
            return stack.enter_context(nc.sbuf_tensor(name, shape, dt))

        def sem(name):
            return ctx.enter_context(nc.semaphore(name))

        ring = sb("ring", [P, SLOTS, SLOT])
        x_t = sb("x_t", [P, KD, T])
        ident = sb("ident", [P, P])
        mean_w = sb("mean_w", [P, P])
        iota = sb("iota", [P, P])
        vecs = sb("vecs", [P, DEPTH * NVEC])
        lv = sb("lv", [P, NVEC])
        st_hi = sb("st_hi", [P, 2, D], F32R)
        st_lo = sb("st_lo", [P, 2, D], F32R)
        c_act = sb("c_act", [P, KD])
        mod = sb("mod", [P, 6 * KD])
        amp = sb("amp", [P, 2, KD])
        g1b = sb("g1b", [P, KD])
        inv_n = sb("inv_n", [P, PADP])
        eps = sb("eps", [P, 1])
        ones = sb("ones", [P, 1])
        own = sb("own", [P, 2, TB * TG])
        own_p = sb("own_p", [P, 2, TB * TG])
        ps = ctx.enter_context(nc.psum_tensor("ps", [P, 8, 512], F32))

        def tile(j):
            return ps[:, j % 4, 0:T]

        def co_tile(j):
            return ps[:, 4 + j % 2, 0:T]

        def pair(j):
            return ps[:, j // 2, (j % 2) * T:(j % 2 + 1) * T]

        def weight_tile(s, j):
            return ring[:, s, :].rearrange("p (k n) -> p k n", k=KD)[:, :, (j % 2) * P:(j % 2 + 1) * P]

        def by_group(v):
            return v.rearrange("p (k n) -> p k n", k=KD)

        mix = ExitStack()
        gates_q = sb("gates_q", [P, HP, T], stack=mix)
        keys_t = sb("keys_t", [P, HP, P], stack=mix)
        h = sb("h", [P, KD, T], stack=mix)
        sq = sb("sq", [P, KD, T], stack=mix)
        scaled = sb("scaled", [P, KD, T], stack=mix)
        u_pad = sb("u_pad", [P, KD, PADC + T], stack=mix)
        conv = sb("conv", [P, KD, T], stack=mix)
        p_pad = sb("p_pad", [P, KD, PADP + T], stack=mix)
        y_parts = ExitStack()
        y_hi = sb("y_hi", [P, KD, T], F32R, stack=y_parts)
        y_lo = sb("y_lo", [P, KD, T], F32R, stack=y_parts)
        y_parts.close()
        win_a = sb("win_a", [P, KD, PADP + T], stack=mix)
        win_b = sb("win_b", [P, KD, PADP + T], stack=mix)
        gate_a, gate_b, q_t = gates_q[:, 0:KD, :], gates_q[:, KD:2 * KD, :], gates_q
        pool_out = sb("pool_out", [P, KD, T], stack=mix)
        val_y = sb("val_y", [P, KD, T], stack=mix)
        keys_n = scaled[:, :, :].rearrange("p k (a n) -> p (k a) n", a=2)
        xn = val_y
        tap_p = scaled[:, 0:2 * KP, :].rearrange("p (b k) t -> p b k t", b=2)
        ada_acc = pool_out[:, :, :].rearrange("p (b k) t -> p b (k t)", b=2)
        ada_acc5 = u_pad[:, :, :].rearrange("p k t -> p (k t)")[:, 0:SEC]
        pw = sb("pw", [P, KD, 2 * P], stack=mix)
        cw_n = sb("cw_n", [124, 2, P], stack=mix)
        cw = sb("cw", [P, 2 * 124], stack=mix)
        root = sb("root", [P, T], stack=mix)
        rs = sb("rs", [P, T], stack=mix)
        rows = sb("rows", [P, 2 * DEPTH, P], stack=mix)
        mix.close()
        gs = sb("gs", [P, CHUNKS * T])
        idx_t = sb("idx_t", [P, 3, T])
        part = ExitStack()
        h_hi = sb("h_hi", [P, KD, T], F32R, stack=part)
        h_lo = sb("h_lo", [P, KD, T], F32R, stack=part)
        part.close()
        hot1 = sb("hot1", [P, 2, TG, P])
        hot2 = sb("hot2", [P, 2, TG, P])
        away = sb("away", [P, 2, TG, P])
        p_hi = sb("p_hi", [P, 2, T], F32R)
        p_lo = sb("p_lo", [P, 2, T], F32R)

        R0 = 96 * T

        def tail(at, n, dt=F32):
            v = gs[:, R0 + at:R0 + at + n]
            return v if dt is F32 else v.bitcast(dt)
        scores = tail(0, TT * HP * P)
        B0 = TT * HP * P
        top_v = tail(B0, 512)
        top_i = tail(B0 + 512, 512)
        logits = tail(B0 + 1024, 256)
        picks = tail(B0 + 1280, 768)
        cand = tail(B0 + 2048, 256)
        cand2 = tail(B0 + 2304, 256)
        pick_hot = tail(B0 + 2560, 256)
        pick_hot2 = tail(B0 + 2816, 256)
        work = tail(B0 + 3072, P)
        work2 = tail(B0 + 3200, P)
        best_v = tail(B0 + 3328, TOPK)
        best_i = tail(B0 + 3344, TOPK, U32)
        pos = tail(B0 + 3360, TOPK, U32)
        pos_f = tail(B0 + 3376, TOPK)
        shifted = tail(B0 + 3392, 256)
        expo = tail(B0 + 3648, 256)
        total = tail(B0 + 3904, TT * HEADS)
        total_r = tail(B0 + 3920, TT * HEADS)
        o_sb = gs[:, 0:TT * D].rearrange("p (a d) -> p a d", a=TT)

        ring_full = [sem(f"ring_full{s}") for s in range(SLOTS)]
        slot_read = [sem(f"slot_read{s}") for s in range(SLOTS)]
        rows_in = sem("rows_in")
        x_in = sem("x_in")
        small_in = sem("small_in")
        out_done = sem("out_done")
        consts_ready = sem("consts_ready")
        start_mm = sem("start_mm")
        vecs_ready = sem("vecs_ready")
        c_ready = sem("c_ready")
        x_ready = sem("x_ready")
        setup_mm = sem("setup_mm")
        setup_ready = sem("setup_ready")
        rs_ready = sem("rs_ready")
        xn_ready = sem("xn_ready")
        h_hi_ready = sem("h_hi_ready")
        ada_part = sem("ada_part")
        ada_mm = sem("ada_mm")
        w_hi = sem("w_hi")
        w_lo = sem("w_lo")
        part_mm = sem("part_mm")
        glu_ready = sem("glu_ready")
        tap_ready = sem("tap_ready")
        tap_added = sem("tap_added")
        sqc_ready = sem("sqc_ready")
        sq2_ready = sem("sq2_ready")
        sum_ready = sem("sum_ready")
        x_hi_ready = sem("x_hi_ready")
        y_out = sem("y_out")
        mod_ready = sem("mod_ready")
        sq_ready = sem("sq_ready")
        mean_mm = sem("mean_mm")
        root_ready = sem("root_ready")
        scaled_ready = sem("scaled_ready")
        h_ready = sem("h_ready")
        x_sum = sem("x_sum")
        x_lo_ready = sem("x_lo_ready")
        z_out = sem("z_out")
        conv_ready = sem("conv_ready")
        cen_mm = sem("cen_mm")
        cen_ready = sem("cen_ready")
        conv_act = sem("conv_act")
        pooled_ready = sem("pooled_ready")
        pool_mm = sem("pool_mm")
        pool_ready = sem("pool_ready")
        y_ready = sem("y_ready")
        res_ready = sem("res_ready")
        q_out = sem("q_out")
        score_mm = sem("score_mm")
        score_a = sem("score_a")
        score_v = sem("score_v")
        ut_mm = sem("ut_mm")
        ut_hi = sem("ut_hi")
        ut_lo = sem("ut_lo")
        s_mm = sem("s_mm")
        s_act = sem("s_act")
        logits_ready = sem("logits_ready")
        expo_ready = sem("expo_ready")
        picks_ready = sem("picks_ready")
        picks_mm = sem("picks_mm")
        idx_ready = sem("idx_ready")
        hot1_ready = sem("hot1_ready")
        hot1_last = sem("hot1_last")
        away_ready = sem("away_ready")
        hot2_ready = sem("hot2_ready")
        w_mm = sem("w_mm")
        w_used = sem("w_used")
        v_hi_ready = sem("v_hi_ready")
        v_lo_ready = sem("v_lo_ready")
        pv_mm = sem("pv_mm")
        o_a = sem("o_a")
        o_v = sem("o_v")
        o_mm = sem("o_mm")
        fin_ready = sem("fin_ready")

        def kview(w):
            return w.rearrange("l (k p) n -> l p k n", p=P)
        ada_v, in_v, co_v, wo_v, wq_v = (kview(w) for w in (ada_w, w_in, w_conv_out, w_out, peer_wq))
        u_v, v_v = (w.rearrange("l (c p) d -> l p c d", p=P) for w in (peer_u, peer_v))
        cw_v = conv_w.rearrange("l k (g p) -> l (k g) p", p=P)
        keys_v = peer_keys.rearrange("l h a n k -> l n (h a) k")
        pw_v = pool_w.rearrange("l g (k p) d -> l p (g k) d", p=P)

        def slot_done(eng, s, l, section, i=0):
            eng.wait_ge(slot_read[s], (l * N_SEC + i) + (section + 2))

        passed = sem("passed")

        def wait_alone(eng, semaphore, value):
            eng.wait_ge(semaphore, value)
            eng.sem_inc(passed, 1)

        block = ctx.enter_context(nc.Block())

        @block.sync
        def _(sp):
            sp.dma_start(val_y[:, :, :].rearrange("p (a k) t -> p a (k t)", a=TT),
                         x[0].rearrange("(a p) d -> p a d", p=P)).then_inc(x_in, 16)

            def load(l, first, i, s, dst, src):
                sp.wait_ge(slot_read[s], (l * N_SEC + i) + (first + 1))
                sp.dma_start(dst, src).then_inc(ring_full[s], 16)

            def stream(l, first, count, source):
                with sp.Fori(0, count) as i:
                    for s in range(SLOTS):
                        load(l, first, i, s, *source(i, s))

            def columns(l, w):
                return lambda i, s: (ring[:, s, :].rearrange("p (k n) -> p k n", k=KD),
                                     w[l, :, :, bass.ds(i * SEC + s * NB, NB)])

            def experts(l, w):
                return lambda i, s: (ring[:, s, :].rearrange("p (c d) -> p c d", c=CPS),
                                     w[l, :, bass.ds(i * CSEC + s * CPS, CPS), :])

            with sp.Fori(0, DEPTH) as l:
                def mixed(first, count, w, sixth):
                    with sp.Fori(0, count) as i:
                        for s in range(SLOTS):
                            src, at = (w, 0) if s < 2 else (ada_v, sixth * SEC)
                            load(l, first, i, s, ring[:, s, :].rearrange("p (k n) -> p k n", k=KD),
                                 src[l, :, :, bass.ds(i * (2 * NB) + (at + s % 2 * NB), NB)])

                def plain(first, w, section):
                    for s in range(SLOTS):
                        load(l, first, 0, s, *columns(l, w)(section, s))

                stream(l, S_ADA01, 2, columns(l, ada_v))
                for i, slots in enumerate(X_SECTIONS):
                    for s, (which, b) in enumerate(slots):
                        w = in_v if which == "in" else ada_v
                        load(l, S_X + i, 0, s, ring[:, s, :].rearrange("p (k n) -> p k n", k=KD),
                             w[l, :, :, b * NB:(b + 1) * NB])
                plain(S_CO, co_v, 0)
                plain(S_OUT, wo_v, 0)
                mixed(S_Y, 2, wq_v, 5)
                plain(S_Q1, wq_v, 1)
                stream(l, S_U, USECS, experts(l, u_v))
                stream(l, S_V, USECS, experts(l, v_v))
            sp.wait_ge(fin_ready, 2)
            sp.dma_start(out[0].rearrange("(a p) d -> p a d", p=P), o_sb).then_inc(out_done, 16)
            sp.wait_ge(out_done, 16)

        @block.gpsimd
        def _(pool):
            pool.memset(ident[:, :], 0.0)
            pool.memset(mean_w[:, :], 1.0 / D)
            pool.memset(eps[:, :], EPS)
            pool.memset(ones[:, :], 1.0)
            for t in range(PADP):
                pool.memset(inv_n[:, t:t + 1], 1.0 / (t + 1))
            pool.iota(iota[:, :], pattern=[[1, P]], base=0, channel_multiplier=0,
                      allow_small_or_imprecise_dtypes=True)
            pool.drain()
            pool.affine_select(out=ident[:, :], in_=ident[:, :], compare_op=ALU.not_equal, fill=1.0,
                               base=0, pattern=[[-1, P]], channel_multiplier=1).then_inc(consts_ready, 1)

            with pool.Fori(0, DEPTH) as l:
                wait_alone(pool, x_ready, l + 1)
                pool.memset(p_pad[:, :, 0:PADP], 0.0)
                pool.wait_ge(rs_ready, l + 1)
                pool.tensor_tensor(xn[:, :, :], x_t[:, :, :], rs[:, :].unsqueeze(1).broadcast_to([P, KD, T]),
                                   ALU.mult).then_inc(xn_ready, 1)
                wait_alone(pool, tap_ready, l * TAPS + 1)
                for tap in range(1, TAPS):
                    pool.wait_ge(tap_ready, l * TAPS + (tap + 1))
                    pool.tensor_tensor(conv[:, KV:KD, :], conv[:, KV:KD, :], tap_p[:, tap % 2, :, :],
                                       ALU.add).then_inc(tap_added, 1)
                    pool.drain()
                wait_alone(pool, z_out, l * (N_IN * KD) + (4 + 3 * KD))
                pool.drain()

                def window(dst, src, g, lo, shift):
                    k = 2 * g
                    end = PADP + T
                    pool.tensor_tensor(dst[:, k:KD, lo:end], src[:, k:KD, lo:end],
                                       src[:, k:KD, lo - shift:end - shift], ALU.add)
                    pool.drain()
                window(win_a, p_pad, 0, 1, 1)
                window(win_b, win_a, 1, 3, 2)
                window(win_a, win_b, 2, 7, 4)
                window(win_b, win_a, 3, 15, 8)
                for g, w in enumerate(WINDOWS):
                    v = (win_a, win_b)[g % 2][:, 2 * g:2 * g + 2, PADP:PADP + T]
                    pool.tensor_scalar(v[:, :, w - 1:T], v[:, :, w - 1:T], 1.0 / w, None, ALU.mult)
                    pool.tensor_tensor(v[:, :, 0:w - 1], v[:, :, 0:w - 1],
                                       inv_n[:, 0:w - 1].unsqueeze(1).broadcast_to([P, 2, w - 1]), ALU.mult)
                pool.drain()
                for g, w in enumerate(WINDOWS):
                    v = (win_a, win_b)[g % 2][:, 2 * g:2 * g + 2, PADP:PADP + T]
                    last = pool.tensor_tensor(v, v,
                                              p_pad[:, 2 * g:2 * g + 2, PADP:PADP + T], ALU.subtract)
                last.then_inc(pooled_ready, 1)
                for j in range(1, KD):
                    pool.wait_ge(sq2_ready, l * KD + (j + 1))
                    last = pool.tensor_tensor(sq[:, 0, :], sq[:, 0, :], sq[:, j, :], ALU.add)
                    if j < KD - 1:
                        pool.drain()
                last.then_inc(sum_ready, 1)

                pool.wait_ge(idx_ready, l + 1)
                wait_alone(pool, s_mm, l * CHUNKS + (CHUNKS + 2))
                with pool.Fori(0, NTG // TB) as i:
                    pool.drain()
                    pool.tensor_copy(own_p[:, :, :], idx_t[:, 0:2, bass.ds(i * (TB * TG), TB * TG)])
                    pool.drain()
                    for n in range(TB):
                        pool.wait_ge(hot2_ready, (l * NTG + i * TB) + (n + 1))
                        pool.tensor_tensor(
                            away[:, n % 2, :, :], iota[:, :].unsqueeze(1).broadcast_to([P, TG, P]),
                            idx_t[:, 2, bass.ds(i * (TB * TG) + n * TG, TG)].unsqueeze(2).broadcast_to([P, TG, P]),
                            ALU.subtract).then_inc(away_ready, 1)
                        wait_alone(pool, w_mm, (l * NTG + i * TB) + (n + 1))
                        t = n * TG + TG - 1
                        pool.tensor_scalar(hot1[:, n % 2, TG - 1, :], iota[:, :], own_p[:, 0, t:t + 1],
                                           own_p[:, 1, t:t + 1], ALU.is_equal, ALU.mult).then_inc(hot1_last, 1)

        @block.scalar
        def _(act):
            for l in range(DEPTH):
                at = 0
                for w, n in ((norm1_g, 8), (b_in, 40), (conv_b, 8), (conv_ln_g, 8), (conv_ln_b, 8),
                             (pool_scale, 8), (b_out, 8), (norm2_g, 8)):
                    act.dma_start(rows[at:at + n, 2 * l, :], w[l].rearrange("(r p) -> r p", p=P)).then_inc(rows_in, 16)
                    at += n
                act.dma_start(rows[0:48, 2 * l + 1, :], ada_b[l].rearrange("(r p) -> r p", p=P)).then_inc(rows_in, 16)
                act.dma_start(rows[48:56, 2 * l + 1, :], c[0].rearrange("(r p) -> r p", p=P)).then_inc(rows_in, 16)
                act.dma_start(rows[56:64, 2 * l + 1, :], final_g.rearrange("(r p) -> r p", p=P)).then_inc(rows_in, 16)
            act.sem_inc(z_out, 4)
            act.sem_inc(hot2_ready, 2)
            act.sem_inc(s_act, 2)
            act.sem_inc(ut_hi, 2)
            act.wait_ge(vecs_ready, 1)
            act.activation(c_act[:, :], vecs[:, V_C:V_C + KD], ACT.Silu).then_inc(c_ready, 1)

            def norm_root(l, n, per):
                act.activation(sq[:, :, :], x_t[:, :, :], ACT.Square).then_inc(sq_ready, 1)
                act.wait_ge(mean_mm, l * per + n)
                act.activation(root[:, :], ps[:, 6, 0:T], ACT.Sqrt, bias=eps[:, 0:1]).then_inc(root_ready, 1)

            def tap_product(l, tap):
                if tap == 0:
                    act.wait_ge(glu_ready, l * KD + KD)
                for k in range(KV, KD if tap < TAPS else KV):
                    w, u = cw[:, tap * KD + k:tap * KD + k + 1], u_pad[:, k, tap:tap + T]
                    if tap == 0:
                        last = act.activation(conv[:, k, :], u, ACT.Identity, bias=lv[:, V_CB + k:V_CB + k + 1], scale=w)
                    else:
                        if k == KV and tap > 2:
                            act.wait_ge(tap_added, l * (TAPS - 1) + (tap - 2))
                        last = act.activation(tap_p[:, tap % 2, k - KV, :], u, ACT.Copy, scale=w)
                    if k == KD - 1:
                        last.then_inc(tap_ready, 1)

            def square(l, j):
                act.wait_ge(x_sum, l * KD + (j + 1))
                act.activation(sq[:, j, :], x_t[:, j, :], ACT.Square).then_inc(sq2_ready, 1)

            def round_w(l, n):
                section, s = place(n)
                if n % 2 == 0:
                    act.wait_ge(ring_full[s], l * (N_SEC * 16) + (section + 1) * 16)
                act.wait_ge(part_mm, l * N_W + (n + 1))
                act.activation(by_group(st_hi[:, n % 2, :]), weight_tile(s, n), ACT.Copy).then_inc(w_hi, 1)

            with act.Fori(0, DEPTH) as l:
                act.wait_ge(x_ready, l + 1)
                for i in range(2):
                    act.dma_start(cw_n[:, i, :], cw_v[l, 124 * i:124 * i + 124, :]).then_inc(small_in, 16)
                for i in range(2):
                    act.dma_start(keys_n[:, KD * i:KD * (i + 1), :],
                                  keys_v[l, :, KD * i:KD * (i + 1), :]).then_inc(small_in, 16)
                act.dma_start(pw[:, :, :], pw_v[l]).then_inc(small_in, 16)
                norm_root(l, 1, 3)
                act.wait_ge(mod_ready, l * 3 + 1)

                act.wait_ge(xn_ready, l + 1)
                for k in range(KD):
                    act.activation(h_hi[:, k, :], xn[:, k, :], ACT.Identity, bias=mod[:, M_SH1 + k:M_SH1 + k + 1],
                                   scale=amp[:, 0, k:k + 1]).then_inc(h_hi_ready, 1)
                round_w(l, 0)
                act.wait_ge(h_ready, l * KD + KD)
                for i, (dst, func) in enumerate(((val_y, ACT.Identity), (sq, ACT.Sigmoid), (p_pad, ACT.Identity),
                                                 (gate_a, ACT.Sigmoid), (gate_b, ACT.Sigmoid))):
                    for j in range(KD):
                        n = i * KD + j
                        if n < W_CO:
                            if n + 1 < W_CO:
                                round_w(l, n + 1)
                            act.wait_ge(part_mm, l * N_W + (n + 3))
                        elif j % 2 == 0:
                            section, s = X_PLACE["in", n // 2]
                            slot_done(act, s, l, section)
                        o = dst[:, j, PADP:PADP + T] if i == 2 else dst[:, j, :]
                        act.activation(o, tile(j), func,
                                       bias=lv[:, V_BIN + n:V_BIN + n + 1]).then_inc(z_out, 1)
                        if n >= W_CO:
                            for tap in (2 * (n - W_CO), 2 * (n - W_CO) + 1):
                                tap_product(l, tap)
                for k in range(KD):
                    act.wait_ge(cen_ready, l * KD + (k + 1))
                    act.activation(sq[:, k, :], conv[:, k, :], ACT.Square).then_inc(sqc_ready, 1)
                round_w(l, W_CO)
                act.wait_ge(mean_mm, l * 3 + 2)
                act.activation(root[:, :], ps[:, 6, 0:T], ACT.Sqrt, bias=eps[:, 0:1]).then_inc(root_ready, 1)
                for k in range(KD):
                    act.wait_ge(scaled_ready, l * (2 * KD) + (k + 1))
                    act.activation(conv[:, k, :], scaled[:, k, :], ACT.Silu, bias=lv[:, V_LB + k:V_LB + k + 1],
                                   scale=lv[:, V_LG + k:V_LG + k + 1]).then_inc(conv_act, 1)
                for n in range(W_CO + 1, W_OUT + 1):
                    round_w(l, n)
                act.wait_ge(mod_ready, l * 3 + 2)
                for j in range(KD):
                    if j + 1 < KD:
                        round_w(l, W_OUT + j + 1)
                    act.wait_ge(part_mm, l * N_W + (W_OUT + j + 3))
                    act.activation(scaled[:, j, :], tile(j), ACT.Identity, bias=g1b[:, j:j + 1],
                                   scale=mod[:, M_G1 + j:M_G1 + j + 1]).then_inc(res_ready, 1)
                    if j:
                        square(l, j - 1)
                square(l, KD - 1)
                act.wait_ge(mean_mm, l * 3 + 3)
                act.activation(root[:, :], ps[:, 6, 0:T], ACT.Sqrt, bias=eps[:, 0:1]).then_inc(root_ready, 1)
                for k in range(KD):
                    act.wait_ge(scaled_ready, l * (2 * KD) + (KD + k + 1))
                    act.activation(h_hi[:, k, :], scaled[:, k, :], ACT.Identity,
                                   bias=mod[:, M_SH2 + k:M_SH2 + k + 1]).then_inc(h_hi_ready, 1)
                round_w(l, W_Q)
                for j in range(HP):
                    if j + 1 < HP:
                        round_w(l, W_Q + j + 1)
                    act.wait_ge(part_mm, l * N_W + (W_Q + j + 3))
                    act.activation(q_t[:, j, :], tile(j), ACT.Copy).then_inc(q_out, 1)
                act.wait_ge(score_mm, l * TT + 2)
                act.activation(scores[:, HP * P:2 * HP * P].rearrange("p (b n) -> p b n", n=512),
                               ps[:, 4:8, :], ACT.Copy).then_inc(score_a, 1)

                def round_u(sec, n):
                    sec, n = sec + n // CSEC, n % CSEC
                    cc, b = sec * CSEC + n, n % 2
                    if b == 0:
                        act.wait_ge(ut_mm, (l * (CHUNKS // 2) + sec * (CSEC // 2)) + (n // 2 + 1))
                    else:
                        slot_done(act, n // CPS, l, S_U, sec)
                    act.wait_ge(s_mm, (l * CHUNKS + cc) + 1)
                    act.activation(st_hi[:, b, :].rearrange("p (a n) -> p a n", a=2),
                                   ps[:, 2 * b:2 * b + 2, :], ACT.Copy).then_inc(ut_hi, 1)

                def gelu(cc, b):
                    act.wait_ge(s_mm, (l * CHUNKS + cc) + 3)
                    act.activation(gs[:, bass.ds(cc * T, T)], ps[:, 4 + b, 0:T], ACT.Gelu).then_inc(s_act, 1)

                def u_section(i, last=False):
                    for n in range(CSEC):
                        if not (last and n == CSEC - 1):
                            round_u(i, n + 1)
                        gelu(i * CSEC + n, n % 2)

                round_u(0, 0)
                with act.Fori(0, 10) as i:
                    u_section(i)
                act.wait_ge(logits_ready, l + 1)
                act.activation(expo, shifted, ACT.Exp).then_inc(expo_ready, 1)
                with act.Fori(10, USECS - 1) as i:
                    u_section(i)
                u_section(USECS - 1, last=True)

                with act.Fori(0, NTG // TB) as i:
                    for n in range(TB):
                        b = n % 2
                        act.wait_ge(away_ready, (l * NTG + i * TB) + (n + 1))
                        act.activation(away[:, b, :, :], away[:, b, :, :], ACT.Abs)
                        act.drain()
                        act.wait_ge(w_mm, (l * NTG + i * TB) + (n + 1))
                        act.activation(hot2[:, b, :, :], away[:, b, :, :], ACT.Relu, bias=1.0,
                                       scale=-1.0).then_inc(hot2_ready, 1)
                act.wait_ge(w_used, l * NTG + (NTG + 2))
                with act.Fori(0, USECS) as i:
                    for n in range(CSEC):
                        b = n % 2
                        if n % CPS == 0:
                            act.wait_ge(ring_full[n // CPS], (l * N_SEC + i) * 16 + (S_V + 1) * 16)
                        act.wait_ge(pv_mm, (l * CHUNKS + i * CSEC) + (n + 1))
                        act.activation(st_hi[:, b, :], ring[:, n // CPS, b * D:(b + 1) * D], ACT.Copy)
                        act.activation(p_hi[:, b, :], gs[:, bass.ds(i * (CSEC * T) + n * T, T)],
                                       ACT.Copy).then_inc(v_hi_ready, 1)
                act.wait_ge(pv_mm, l * CHUNKS + (CHUNKS + 2))
                act.activation(o_sb[:, 0, :].rearrange("p (a n) -> p a n", a=2), ps[:, 0:2, :], ACT.Copy).then_inc(o_a, 1)

            act.wait_ge(x_ready, DEPTH + 1)
            norm_root(0, 3 * DEPTH + 1, 0)
            act.wait_ge(o_mm, DEPTH + 1)
            act.activation(o_sb[:, 0, :].rearrange("p (a n) -> p a n", a=2), ps[:, 0:2, :], ACT.Copy).then_inc(fin_ready, 1)

        @block.vector
        def _(dve):
            dve.sem_inc(ut_lo, 2)
            dve.sem_inc(w_used, 2)
            dve.wait_ge(start_mm, 1)
            for l in range(DEPTH):
                dve.tensor_copy(vecs[:, l * NVEC:l * NVEC + ROWS_A], ps[:, 2 * l, 0:ROWS_A])
                last = dve.tensor_copy(vecs[:, l * NVEC + ROWS_A:(l + 1) * NVEC], ps[:, 2 * l + 1, 0:ROWS_B])
            last.then_inc(vecs_ready, 1)
            dve.wait_ge(start_mm, 2)
            dve.tensor_copy(x_t[:, :, :].rearrange("p (b c) t -> p b (c t)", c=2), ps[:, 4:8, :]).then_inc(x_ready, 1)

            def norm_scale(l, n, gain):
                dve.wait_ge(root_ready, n)
                dve.reciprocal(rs[:, :], root[:, :])
                dve.drain()
                for k in range(KD):
                    dve.scalar_tensor_tensor(scaled[:, k, :], x_t[:, k, :], gain(k), rs[:, :], ALU.mult,
                                             ALU.mult).then_inc(scaled_ready, 1)

            wait_alone(dve, c_ready, 1)
            with dve.Fori(0, DEPTH) as l:
                dve.wait_ge(x_ready, l + 1)
                dve.tensor_copy(lv[:, :], vecs[:, bass.ds(l * NVEC, NVEC)])
                dve.memset(u_pad[:, :, 0:PADC], 0.0)
                def ada_steps(section, s, dst, ks=range(KD)):
                    o = dst.rearrange("p (s n) -> p s n", s=2)
                    for k in ks:
                        w = ring[:, s:s + 2, k * NB:(k + 1) * NB]
                        if k == 0:
                            dve.wait_ge(ring_full[s], l * (N_SEC * 16) + (section + 1) * 16)
                            dve.wait_ge(ring_full[s + 1], l * (N_SEC * 16) + (section + 1) * 16)
                            last = dve.tensor_scalar(o, w, c_act[:, 0:1], None, ALU.mult)
                        else:
                            dve.drain()
                            last = dve.scalar_tensor_tensor(o, w, c_act[:, k:k + 1], o, ALU.mult, ALU.add)
                        if k == KD - 1:
                            last.then_inc(slot_read[s], 1)
                            dve.drain().then_inc(slot_read[s + 1], 1)
                            dve.drain().then_inc(ada_part, 1)

                def ada_half(a, q):
                    acc = ada_acc5 if a == 5 else ada_acc[:, a % 2, :]
                    return acc[:, q * 2 * NB:(q + 1) * 2 * NB]

                def ada_between(n, at, section, s, dst):
                    if at <= n < at + 4:
                        ada_steps(section, s, dst, (2 * (n - at), 2 * (n - at) + 1))

                def rest_w(n):
                    section, s = place(n)
                    dve.wait_ge(w_hi, l * N_W + (n + 1))
                    dve.tensor_tensor(by_group(st_lo[:, n % 2, :]), weight_tile(s, n),
                                      by_group(st_hi[:, n % 2, :]).bitcast(F32),
                                      ALU.subtract).then_inc(slot_read[s] if n % 2 else w_lo, 1)

                def take_mod(a0, a1):
                    dve.wait_ge(ada_mm, l * (2 * N_ADA) + 2 * a1)
                    dve.tensor_tensor(mod[:, a0 * KD:a1 * KD], ps[:, 7, a0 * KD:a1 * KD],
                                      lv[:, V_ADAB + a0 * KD:V_ADAB + a1 * KD], ALU.add)
                    dve.drain()

                ada_steps(S_ADA01, 0, ada_half(0, 0))
                ada_steps(S_ADA01, 2, ada_half(0, 1))
                ada_steps(S_ADA01 + 1, 0, ada_half(1, 0))
                dve.wait_ge(root_ready, l * 3 + 1)
                dve.reciprocal(rs[:, :], root[:, :]).then_inc(rs_ready, 1)
                ada_steps(S_ADA01 + 1, 2, ada_half(1, 1))
                dve.wait_ge(setup_mm, l + 1)
                dve.tensor_copy(cw[:, :], ps[:, 4, 0:2 * 124])
                dve.tensor_copy(keys_t[:, :, :].rearrange("p (b c) n -> p b (c n)", c=4), ps[:, 0:4, :]).then_inc(setup_ready, 1)
                take_mod(0, 2)
                dve.scalar_tensor_tensor(amp[:, 0, :], mod[:, M_SC1:M_SC1 + KD], 1.0, lv[:, V_N1:V_N1 + KD], ALU.add,
                                         ALU.mult).then_inc(mod_ready, 1)
                dve.drain()
                dve.wait_ge(xn_ready, l + 1)
                for k in range(KD):
                    dve.tensor_scalar(h[:, k, :], xn[:, k, :], amp[:, 0, k:k + 1],
                                      mod[:, M_SH1 + k:M_SH1 + k + 1], ALU.mult, ALU.add).then_inc(h_ready, 1)
                dve.drain()
                for k in range(KD):
                    dve.wait_ge(h_hi_ready, l * (2 * KD) + (k + 1))
                    last = dve.tensor_tensor(h_lo[:, k, :], h[:, k, :], h_hi[:, k, :].bitcast(F32), ALU.subtract)
                last.then_inc(x_lo_ready, 1)
                for n in range(W_CO):
                    rest_w(n)
                    ada_between(n, 1, *X_PLACE["ada", 8], ada_half(2, 0))
                    ada_between(n, 9, *X_PLACE["ada", 10], ada_half(2, 1))
                for j in range(KD):
                    dve.wait_ge(z_out, l * (N_IN * KD) + (4 + KD + j + 1))
                    dve.tensor_tensor(u_pad[:, j, PADC:PADC + T], val_y[:, j, :], sq[:, j, :], ALU.mult).then_inc(glu_ready, 1)
                dve.drain()
                for k in range(KV):
                    dve.tensor_scalar(conv[:, k, :], u_pad[:, k, 0:T], cw[:, k:k + 1],
                                      lv[:, V_CB + k:V_CB + k + 1], ALU.mult, ALU.add)
                for first, end, a, q in ((1, 6, 3, 0), (6, 14, 3, 1), (14, 22, 4, 0), (22, 26, 4, 1),
                                         (26, TAPS - 1, None, None)):
                    with dve.Fori(first, end) as tap:
                        dve.drain()
                        for k in range(KV):
                            dve.scalar_tensor_tensor(conv[:, k, :], u_pad[:, k, bass.ds(tap, T)],
                                                     cw[:, bass.ds(tap * KD + k, 1)], conv[:, k, :], ALU.mult, ALU.add)
                    if a:
                        if (a, q) == (4, 0):
                            dve.wait_ge(ada_mm, l * (2 * N_ADA) + 6)
                        ada_steps(*X_PLACE["ada", 4 * a + 2 * q], ada_half(a, q))
                dve.drain()
                for k in range(KV):
                    dve.scalar_tensor_tensor(conv[:, k, :], u_pad[:, k, TAPS - 1:TAPS - 1 + T],
                                             cw[:, (TAPS - 1) * KD + k:(TAPS - 1) * KD + k + 1], conv[:, k, :],
                                             ALU.mult, ALU.add).then_inc(conv_ready, 1)
                dve.wait_ge(cen_mm, l + 1)
                for k in range(KD):
                    dve.tensor_tensor(conv[:, k, :], conv[:, k, :], ps[:, 5, 0:T], ALU.subtract).then_inc(cen_ready, 1)
                dve.wait_ge(root_ready, l * 3 + 2)
                dve.reciprocal(rs[:, :], root[:, :])
                dve.drain()
                for k in range(KD):
                    dve.tensor_tensor(scaled[:, k, :], conv[:, k, :], rs[:, :], ALU.mult).then_inc(scaled_ready, 1)
                rest_w(W_CO)
                for k in range(KD):
                    dve.wait_ge(conv_act, l * KD + (k + 1))
                    dve.tensor_copy(h_hi[:, k, :], conv[:, k, :]).then_inc(x_hi_ready, 1)
                dve.drain()
                dve.tensor_tensor(h_lo[:, :, :], conv[:, :, :], h_hi[:, :, :].bitcast(F32), ALU.subtract).then_inc(x_lo_ready, 1)
                for j in range(KD):
                    if j % 2 == 0:
                        dve.wait_ge(pool_mm, l * (KD // 2) + (j // 2 + 1))
                    dve.scalar_tensor_tensor(pool_out[:, j, :], pair(j),
                                             lv[:, V_PS + j:V_PS + j + 1], gate_b[:, j, :], ALU.mult,
                                             ALU.mult).then_inc(pool_ready, 1)
                for j in range(KD):
                    if j + 1 < KD:
                        rest_w(W_CO + j + 1)
                    dve.wait_ge(part_mm, l * N_W + (W_CO + j + 3))
                    dve.tensor_tensor(val_y[:, j, :], co_tile(j), gate_a[:, j, :], ALU.mult).then_inc(y_out, 1)
                    dve.drain()
                    dve.tensor_tensor(val_y[:, j, :], val_y[:, j, :], pool_out[:, j, :], ALU.add)
                    dve.drain()
                    dve.tensor_copy(y_hi[:, j, :], val_y[:, j, :]).then_inc(x_hi_ready, 1)
                    dve.drain()
                    last = dve.tensor_tensor(y_lo[:, j, :], val_y[:, j, :], y_hi[:, j, :].bitcast(F32), ALU.subtract)
                last.then_inc(x_lo_ready, 1)
                rest_w(W_OUT)
                take_mod(2, 5)
                dve.tensor_tensor(g1b[:, :], mod[:, M_G1:M_G1 + KD], lv[:, V_BO:V_BO + KD], ALU.mult)
                dve.scalar_tensor_tensor(amp[:, 1, :], mod[:, M_SC2:M_SC2 + KD], 1.0, lv[:, V_N2:V_N2 + KD],
                                         ALU.add, ALU.mult).then_inc(mod_ready, 1)
                for j in range(KD):
                    if j + 1 < KD:
                        rest_w(W_OUT + j + 1)
                    dve.wait_ge(res_ready, l * KD + (j + 1))
                    dve.tensor_tensor(x_t[:, j, :], x_t[:, j, :], scaled[:, j, :], ALU.add).then_inc(x_sum, 1)
                norm_scale(l, l * 3 + 3, lambda k: amp[:, 1, k:k + 1])
                for k in range(KD):
                    dve.wait_ge(h_hi_ready, l * (2 * KD) + (KD + k + 1))
                    last = dve.scalar_tensor_tensor(h_lo[:, k, :], scaled[:, k, :], mod[:, M_SH2 + k:M_SH2 + k + 1],
                                                    h_hi[:, k, :].bitcast(F32), ALU.add, ALU.subtract)
                last.then_inc(x_lo_ready, 1)
                for n in range(HP):
                    rest_w(W_Q + n)
                    ada_between(n, 2, S_Y, 2, ada_half(5, 0))
                    ada_between(n, 6, S_Y + 1, 2, ada_half(5, 1))
                take_mod(5, 6)
                dve.drain().then_inc(mod_ready, 1)
                dve.wait_ge(score_mm, l * TT + 1)
                dve.tensor_copy(scores[:, 0:HP * P].rearrange("p (b n) -> p b n", n=512), ps[:, 0:4, :]).then_inc(score_v, 1)
                wait_alone(dve, score_a, l + 1)

                def rest_u(cc, b):
                    dve.wait_ge(ut_hi, (l * CHUNKS + cc) + 3)
                    dve.tensor_tensor(st_lo[:, b, :].rearrange("p (a n) -> p a n", a=2), ps[:, 2 * b:2 * b + 2, :],
                                      st_hi[:, b, :].bitcast(F32).rearrange("p (a n) -> p a n", a=2),
                                      ALU.subtract).then_inc(ut_lo, 1)

                def top16(values, spare, n_idx):
                    dve.max(best_v[:, 0:8], values)
                    dve.drain()
                    dve.match_replace(out=spare, in_to_replace=best_v[:, 0:8], in_values=values, imm_value=NEG)
                    dve.max_index(n_idx[:, 0:8], best_v[:, 0:8], values)
                    dve.drain()
                    dve.max(best_v[:, 8:16], spare)
                    dve.drain()
                    dve.max_index(n_idx[:, 8:16], best_v[:, 8:16], spare)
                    dve.drain()

                with dve.Fori(0, 4) as i:
                    for n in range(CSEC):
                        rest_u(i * CSEC + n, n % 2)
                        dve.tensor_copy(work, scores[:, bass.ds(i * (CSEC * P) + n * P, P)])
                        dve.drain()
                        top16(work, work2, best_i)
                        dve.tensor_copy(top_v[:, bass.ds(i * (CSEC * TOPK) + n * TOPK, TOPK)], best_v)
                        dve.tensor_copy(top_i[:, bass.ds(i * (CSEC * TOPK) + n * TOPK, TOPK)], best_i)
                dve.drain()
                with dve.Fori(0, 8) as i:
                    for n in range(6):
                        rest_u(i * 6 + (4 * CSEC + n), n % 2)
                        at = i * (4 * TOPK) + (n // 3) * 2 * TOPK
                        th = i * (2 * TOPK) + (n // 3) * TOPK
                        if n % 3 == 0:
                            dve.tensor_tensor(
                                cand.rearrange("p (i j) -> p i j", i=TOPK),
                                top_v[:, bass.ds(at, TOPK)].unsqueeze(2).broadcast_to([P, TOPK, TOPK]),
                                top_v[:, bass.ds(at + TOPK, TOPK)].unsqueeze(1).broadcast_to([P, TOPK, TOPK]), ALU.add)
                            dve.drain()
                            top16(cand, cand2, best_i)
                            dve.tensor_copy(logits[:, bass.ds(th, TOPK)], best_v)
                        else:
                            half = n % 3 - 1
                            a, op = ((4, ALU.logical_shift_right), (TOPK - 1, ALU.bitwise_and))[half]
                            dve.tensor_scalar(pos, best_i, a, None, op)
                            dve.drain()
                            dve.tensor_copy(pos_f, pos)
                            dve.drain()
                            hot = pick_hot.rearrange("p (k j) -> p k j", k=TOPK)
                            hot_b = pick_hot2.rearrange("p (k j) -> p k j", k=TOPK)
                            dve.tensor_tensor(hot, pos_f.unsqueeze(2).broadcast_to([P, TOPK, TOPK]),
                                              iota[:, 0:TOPK].unsqueeze(1).broadcast_to([P, TOPK, TOPK]), ALU.is_equal)
                            dve.drain()
                            dve.tensor_tensor(hot_b, hot, top_i[:, bass.ds(at + half * TOPK, TOPK)].unsqueeze(1)
                                              .broadcast_to([P, TOPK, TOPK]), ALU.mult)
                            dve.drain()
                            dve.tensor_reduce(picks[:, bass.ds(th + half * (2 * T), TOPK)], hot_b, axis=AX.X, op=ALU.add)
                dve.drain()
                by_head = dict(k=TOPK)
                dve.tensor_tensor(shifted.rearrange("p (g k) -> p g k", **by_head),
                                  logits.rearrange("p (g k) -> p g k", **by_head),
                                  logits.rearrange("p (g k) -> p g k", **by_head)[:, :, 0:1].broadcast_to(
                                      [P, TT * HEADS, TOPK]), ALU.subtract).then_inc(logits_ready, 1)
                with dve.Fori(0, CSEC // 2) as i:
                    for n in range(2):
                        rest_u(i * 2 + (10 * CSEC + n), n)
                dve.wait_ge(expo_ready, l + 1)
                dve.tensor_reduce(total, expo.rearrange("p (g k) -> p g k", **by_head), axis=AX.X, op=ALU.add)
                dve.drain()
                dve.reciprocal(total_r, total)
                dve.drain()
                dve.tensor_tensor(picks[:, T:2 * T].rearrange("p (g k) -> p g k", **by_head),
                                  expo.rearrange("p (g k) -> p g k", **by_head),
                                  total_r.unsqueeze(2).broadcast_to([P, TT * HEADS, TOPK]), ALU.mult).then_inc(picks_ready, 1)
                with dve.Fori(0, CSEC // 2) as i:
                    for n in range(2):
                        rest_u(i * 2 + (11 * CSEC + n), n)
                dve.wait_ge(picks_mm, l + 1)
                dve.tensor_copy(idx_t[:, 0:2, :], ps[:, 6, :].rearrange("p (a t) -> p a t", a=2))
                dve.tensor_copy(idx_t[:, 2, :], ps[:, 7, 0:T]).then_inc(idx_ready, 1)
                with dve.Fori(12, USECS) as i:
                    for n in range(CSEC):
                        rest_u(i * CSEC + n, n % 2)

                def own_rows(first, n):
                    dve.drain()
                    dve.tensor_copy(own[:, :, 0:n], idx_t[:, 0:2, bass.ds(first, n)])
                    dve.drain()

                def hot_rows(n):
                    for k in range(TG - 1):
                        t = n * TG + k
                        last = dve.tensor_scalar(hot1[:, n % 2, k, :], iota[:, :], own[:, 0, t:t + 1],
                                                 own[:, 1, t:t + 1], ALU.is_equal, ALU.mult)
                    last.then_inc(hot1_ready, 1)

                def weigh(g, b):
                    dve.wait_ge(w_mm, (l * NTG + g) + 3)
                    acts = gs[:, :].rearrange("p (c t) -> p t c", t=T)[:, bass.ds(g * TG, TG), :]
                    dve.tensor_tensor(acts, acts, ps[:, b, :].rearrange("p (t c) -> p t c", t=TG),
                                      ALU.mult).then_inc(w_used, 1)

                own_rows(0, 2 * TG)
                dve.wait_ge(s_act, l * CHUNKS + (CHUNKS + 2))
                hot_rows(0)
                hot_rows(1)
                with dve.Fori(0, NTG // TB - 1) as i:
                    own_rows(i * (TB * TG) + 2 * TG, TB * TG)
                    for n in range(TB):
                        weigh(i * TB + n, n % 2)
                        hot_rows(n)
                own_rows(T - 2 * TG, 2 * TG)
                for n in range(TB):
                    weigh(NTG - TB + n, n % 2)
                    if n < 2:
                        hot_rows(n)
                dve.drain()

                with dve.Fori(0, USECS) as i:
                    for n in range(CSEC):
                        b = n % 2
                        dve.wait_ge(v_hi_ready, (l * CHUNKS + i * CSEC) + (n + 1))
                        v = dve.tensor_tensor(st_lo[:, b, :], ring[:, n // CPS, b * D:(b + 1) * D],
                                              st_hi[:, b, :].bitcast(F32), ALU.subtract)
                        if b == CPS - 1:
                            v.then_inc(slot_read[n // CPS], 1)
                        dve.tensor_tensor(p_lo[:, b, :], gs[:, bass.ds(i * (CSEC * T) + n * T, T)],
                                          p_hi[:, b, :].bitcast(F32), ALU.subtract).then_inc(v_lo_ready, 1)
                dve.wait_ge(pv_mm, l * CHUNKS + (CHUNKS + 2))
                dve.tensor_copy(o_sb[:, 1, :].rearrange("p (a n) -> p a n", a=2), ps[:, 2:4, :]).then_inc(o_v, 1)
                dve.wait_ge(o_mm, l + 1)
                for k in range(KD):
                    last = dve.scalar_tensor_tensor(x_t[:, k, :], ps[:, 4 + k // 2, (k % 2) * T:(k % 2 + 1) * T],
                                                    mod[:, M_G2 + k:M_G2 + k + 1], x_t[:, k, :], ALU.mult, ALU.add)
                last.then_inc(x_ready, 1)

            norm_scale(0, 3 * DEPTH + 1, lambda k: vecs[:, V_FG + k:V_FG + k + 1])
            dve.wait_ge(o_mm, DEPTH + 1)
            dve.tensor_copy(o_sb[:, 1, :].rearrange("p (a n) -> p a n", a=2), ps[:, 2:4, :]).then_inc(fin_ready, 1)

        @block.tensor
        def _(pe):
            for s in range(SLOTS):
                pe.sem_inc(slot_read[s], 1)
            pe.sem_inc(part_mm, 2)
            pe.sem_inc(s_mm, 2)
            pe.sem_inc(w_mm, 2)
            pe.sem_inc(pv_mm, 2)
            pe.wait_ge(consts_ready, 1)
            pe.wait_ge(rows_in, 16 * 11 * DEPTH)
            for l in range(DEPTH):
                pe.transpose(ps[:, 2 * l, 0:ROWS_A], rows[0:ROWS_A, 2 * l, :], ident[0:ROWS_A, 0:ROWS_A])
                last = pe.transpose(ps[:, 2 * l + 1, 0:ROWS_B], rows[0:ROWS_B, 2 * l + 1, :], ident[0:ROWS_B, 0:ROWS_B])
            last.then_inc(start_mm, 1)
            pe.wait_ge(x_in, 16)
            xin = val_y[:, :, :].rearrange("p (a k) t -> p a (k t)", a=TT)

            def to_channels(src):
                for k in range(KD):
                    for a in range(TT):
                        last = pe.transpose(ps[:, 4 + k // 2, (k % 2) * T + a * P:(k % 2) * T + (a + 1) * P],
                                            src[:, a, k * P:(k + 1) * P], ident[:, :])
                return last
            to_channels(xin).then_inc(start_mm, 1)
            pe.wait_ge(c_ready, 1)

            def mean_of(src, bank, before=lambda k: None, first=0):
                for k in range(KD):
                    before(k)
                    last = pe.matmul(ps[:, bank, 0:T], mean_w[:, :], src[:, (first + k) % KD, :], start=(k == 0),
                                     stop=(k == KD - 1))
                return last

            def ada_sum(l, a):
                acc = ada_acc5 if a == 5 else ada_acc[:, a % 2, :]
                for q in range(2):
                    pe.wait_ge(ada_part, l * (2 * N_ADA) + (2 * a + q + 1))
                    for j in range(q * KD // 2, (q + 1) * KD // 2):
                        last = pe.matmul(ps[:, 7, a * KD + j:a * KD + j + 1], acc[:, j * P:(j + 1) * P], ones[:, 0:1],
                                         start=True, stop=True)
                    last.then_inc(ada_mm, 1)

            def split_tile(l, n, before=None, x_hi=h_hi, x_lo=h_lo, out=None):
                b, (section, s) = n % 2, place(n)
                out = tile(n) if out is None else out
                pe.wait_ge(w_hi, l * N_W + (n + 1))
                if before:
                    before()
                for k in range(KD):
                    pe.matmul(out, st_hi[:, b, k * P:(k + 1) * P], x_hi[:, k, :], start=(k == 0), stop=False)
                if b:
                    slot_done(pe, s, l, section)
                else:
                    pe.wait_ge(w_lo, l * (N_W // 2) + (n // 2 + 1))
                for k in range(KD):
                    pe.matmul(out, st_lo[:, b, k * P:(k + 1) * P], x_hi[:, k, :], start=False, stop=False)
                pe.wait_ge(x_lo_ready, l * 4 + (1 if n < W_CO else 2 if n < W_OUT else 3 if n < W_Q else 4))
                for k in range(KD):
                    last = pe.matmul(out, st_hi[:, b, k * P:(k + 1) * P], x_lo[:, k, :], start=False,
                                     stop=(k == KD - 1))
                last.then_inc(part_mm, 1)

            with pe.Fori(0, DEPTH) as l:
                pe.wait_ge(sq_ready, l + 1)
                mean_of(sq, 6).then_inc(mean_mm, 1)
                pe.wait_ge(small_in, l * (5 * 16) + 5 * 16)
                for j in range(HP):
                    pe.transpose(ps[:, j // 4, (j % 4) * P:(j % 4 + 1) * P], keys_n[:, j, :], ident[:, :])
                for i in range(2):
                    last = pe.transpose(ps[:, 4, i * 124:(i + 1) * 124], cw_n[:, i, :], ident[0:124, 0:124])
                last.then_inc(setup_mm, 1)
                ada_sum(l, 0)
                ada_sum(l, 1)
                pe.wait_ge(setup_ready, l + 1)
                pe.wait_ge(h_hi_ready, l * (2 * KD) + KD)
                for n in range(W_CO):
                    split_tile(l, n, lambda: pe.wait_ge(z_out, l * (N_IN * KD) + (n + 1)))
                ada_sum(l, 2)
                pe.wait_ge(h_ready, l * KD + KD)
                for n in range(W_CO, N_IN * KD):
                    section, s = X_PLACE["in", n // 2]
                    if n % 2 == 0:
                        pe.wait_ge(ring_full[s], l * (N_SEC * 16) + (section + 1) * 16)
                    pe.wait_ge(z_out, l * (N_IN * KD) + (n + 1))
                    for k in range(KD):
                        at = k * NB + n % 2 * P
                        last = pe.matmul(tile(n), ring[:, s, at:at + P], h[:, k, :], start=(k == 0), stop=(k == KD - 1))
                    if n % 2:
                        last.then_inc(slot_read[s], 1)
                pe.wait_ge(tap_added, l * (TAPS - 1) + (TAPS - 1))
                mean_of(conv, 5, lambda k: k < KP or pe.wait_ge(conv_ready, l * KV + (k - KP + 1)), KV).then_inc(cen_mm, 1)
                ada_sum(l, 3)
                mean_of(sq, 6, lambda k: pe.wait_ge(sqc_ready, l * KD + (k + 1))).then_inc(mean_mm, 1)
                ada_sum(l, 4)
                pe.wait_ge(pooled_ready, l + 1)
                pe.wait_ge(z_out, l * (N_IN * KD) + (N_IN * KD + 4))
                for j in range(KD):
                    g, half = j // 2, j % 2
                    for k in range(2):
                        last = pe.matmul(pair(j),
                                         pw[:, 2 * g + k, half * P:(half + 1) * P],
                                         (win_a, win_b)[g % 2][:, 2 * g + k, PADP:PADP + T],
                                         start=(k == 0), stop=(k == 1))
                    if half:
                        last.then_inc(pool_mm, 1)
                pe.wait_ge(x_hi_ready, l * (2 * KD) + KD)

                def bank_of(sem_, n, banks):
                    return (lambda: pe.wait_ge(sem_, l * KD + (n % KD - banks + 1))) if n % KD >= banks else None
                for n in range(W_CO, W_OUT):
                    split_tile(l, n, bank_of(y_out, n, 2), out=co_tile(n))
                pe.wait_ge(pool_ready, l * KD + KD)
                pe.wait_ge(x_hi_ready, l * (2 * KD) + 2 * KD)
                for n in range(W_OUT, W_Q):
                    split_tile(l, n, bank_of(res_ready, n, 4), y_hi, y_lo)
                pe.wait_ge(sum_ready, l + 1)
                pe.matmul(ps[:, 6, 0:T], mean_w[:, :], sq[:, 0, :], start=True, stop=True).then_inc(mean_mm, 1)
                pe.wait_ge(h_hi_ready, l * (2 * KD) + 2 * KD)
                for n in range(HP):
                    split_tile(l, W_Q + n, (lambda: pe.wait_ge(q_out, l * HP + (n - 3))) if n >= 4 else None)
                pe.wait_ge(mod_ready, l * 3 + 2)
                ada_sum(l, 5)
                pe.wait_ge(q_out, l * HP + HP)
                pe.wait_ge(mod_ready, l * 3 + 3)
                for a in range(TT):
                    for j in range(HP):
                        last = pe.matmul(ps[:, 4 * a + j // 4, (j % 4) * P:(j % 4 + 1) * P],
                                         q_t[:, j, a * P:(a + 1) * P], keys_t[:, j, :], start=True, stop=True)
                    last.then_inc(score_mm, 1)
                pe.wait_ge(score_v, l + 1)
                pe.wait_ge(score_a, l + 1)

                def turn_u(sec, n):
                    sec, n = sec + n // CSEC, n % CSEC
                    cc, b, s = sec * CSEC + n, n % 2, n // CPS
                    if n % CPS == 0:
                        pe.wait_ge(ring_full[s], (l * N_SEC + sec) * 16 + (S_U + 1) * 16)
                    pe.wait_ge(ut_hi, (l * CHUNKS + cc) + 1)
                    pe.wait_ge(ut_lo, (l * CHUNKS + cc) + 1)
                    for k in range(KD):
                        last = pe.transpose(ps[:, 2 * b + k // 4, (k % 4) * P:(k % 4 + 1) * P],
                                            ring[:, s, b * D + k * P:b * D + (k + 1) * P], ident[:, :])
                    last.then_inc(slot_read[s] if b == CPS - 1 else ut_mm, 1)

                def use_u(sec, n):
                    cc, b = sec * CSEC + n, n % 2
                    o = ps[:, 4 + b, 0:T]
                    pe.wait_ge(s_act, (l * CHUNKS + cc) + 1)
                    pe.wait_ge(ut_hi, (l * CHUNKS + cc) + 3)
                    for k in range(KD):
                        pe.matmul(o, st_hi[:, b, k * P:(k + 1) * P], h_hi[:, k, :], start=(k == 0), stop=False)
                        pe.matmul(o, st_hi[:, b, k * P:(k + 1) * P], h_lo[:, k, :], start=False, stop=False)
                    pe.wait_ge(ut_lo, (l * CHUNKS + cc) + 3)
                    for k in range(KD):
                        last = pe.matmul(o, st_lo[:, b, k * P:(k + 1) * P], h_hi[:, k, :], start=False, stop=(k == KD - 1))
                    last.then_inc(s_mm, 1)

                def u_section(i, last=False):
                    for n in range(CSEC):
                        if not (last and n == CSEC - 1):
                            turn_u(i, n + 1)
                        use_u(i, n)
                turn_u(0, 0)
                with pe.Fori(0, 12) as i:
                    u_section(i)
                pe.wait_ge(picks_ready, l + 1)
                for a in range(3):
                    for t in range(TT):
                        last = pe.transpose(ps[:, 6 + a // 2, (a % 2) * T + t * P:(a % 2) * T + (t + 1) * P],
                                            picks[:, a * T + t * P:a * T + (t + 1) * P], ident[:, :])
                last.then_inc(picks_mm, 1)
                with pe.Fori(12, USECS - 1) as i:
                    u_section(i)
                u_section(USECS - 1, last=True)

                with pe.Fori(0, NTG // TB) as i:
                    for n in range(TB):
                        b = n % 2
                        pe.wait_ge(w_used, (l * NTG + i * TB) + (n + 1))
                        pe.wait_ge(hot1_ready, (l * NTG + i * TB) + (n + 1))
                        pe.wait_ge(hot1_last, (l * NTG + i * TB) + (n + 1))
                        pe.wait_ge(hot2_ready, (l * NTG + i * TB) + (n + 3))
                        for k in range(TG):
                            last = pe.matmul(ps[:, b, k * P:(k + 1) * P], hot2[:, b, k, :], hot1[:, b, k, :],
                                             start=True, stop=True)
                        last.then_inc(w_mm, 1)

                pe.wait_ge(w_used, l * NTG + (NTG + 2))

                def v_section(i, first=False, final=False):
                    for n in range(CSEC):
                        b = n % 2
                        start, stop = first and n == 0, final and n == CSEC - 1
                        pe.wait_ge(v_hi_ready, (l * CHUNKS + i * CSEC) + (n + 1))
                        for a in range(TT):
                            for hf in range(2):
                                pe.matmul(ps[:, 2 * a + hf, :], p_hi[:, b, a * P:(a + 1) * P],
                                          st_hi[:, b, hf * 512:(hf + 1) * 512], start=start, stop=False)
                        pe.wait_ge(v_lo_ready, (l * CHUNKS + i * CSEC) + (n + 1))
                        for a in range(TT):
                            for hf in range(2):
                                pe.matmul(ps[:, 2 * a + hf, :], p_hi[:, b, a * P:(a + 1) * P],
                                          st_lo[:, b, hf * 512:(hf + 1) * 512], start=False, stop=False)
                            for hf in range(2):
                                last = pe.matmul(ps[:, 2 * a + hf, :], p_lo[:, b, a * P:(a + 1) * P],
                                                 st_hi[:, b, hf * 512:(hf + 1) * 512], start=False, stop=stop)
                        last.then_inc(pv_mm, 1)
                v_section(0, first=True)
                with pe.Fori(1, USECS - 1) as i:
                    v_section(i)
                v_section(USECS - 1, final=True)
                pe.wait_ge(o_a, l + 1)
                pe.wait_ge(o_v, l + 1)
                to_channels(o_sb).then_inc(o_mm, 1)

            pe.wait_ge(sq_ready, DEPTH + 1)
            mean_of(sq, 6).then_inc(mean_mm, 1)
            for k in range(KD):
                pe.wait_ge(scaled_ready, DEPTH * 2 * KD + k + 1)
                for a in range(TT):
                    last = pe.transpose(ps[:, 2 * a + k // 4, (k % 4) * P:(k % 4 + 1) * P],
                                        scaled[:, k, a * P:(a + 1) * P], ident[:, :])
            last.then_inc(o_mm, 1)


_INS = ["x", "c", "ada_w", "ada_b", "norm1_g", "w_in", "b_in", "conv_w", "conv_b", "conv_ln_g", "conv_ln_b",
        "w_conv_out", "pool_w", "pool_scale", "w_out", "b_out", "norm2_g", "peer_wq", "peer_keys", "peer_u",
        "peer_v", "final_g"]


def kernel(**inputs):
    import concourse.bacc as bacc
    from concourse.bass_utils import run_bass_kernel_spmd

    nc = bacc.Bacc("TRN2", target_bir_lowering=False, num_devices=1)
    arrays, args = {}, []
    for name in _INS:
        a = np.ascontiguousarray(inputs[name])
        arrays[f"in_{name}"] = a
        args.append(nc.dram_tensor(f"in_{name}", a.shape, mybir.dt.from_np(a.dtype), kind="ExternalInput").ap())
    args.append(nc.dram_tensor("out_x", (1, T, D), F32, kind="ExternalOutput").ap())
    build(nc, *args)
    r = run_bass_kernel_spmd(nc, [arrays], core_ids=[0])
    return r.results[0]["out_x"]
```
